# Optimizing a Trainium2 kernel written in Bass

```python
import math
import jax, jax.numpy as jnp
from jax import lax
import numpy as np

D_MODEL = 2048
BATCH = 1
SEQ = 256
DEPTH = 1
DEC_BATCH = 8
DEC_SEQ = 4
PAST_LEN = 2048
PAGE_SIZE = 128

N_HEADS = 8
HEAD_DIM = 128
ATTN_WIDTH = N_HEADS * HEAD_DIM
IDX_HEADS = 16
IDX_DIM = 64
TOPK_MAX = 256
CONV_WIDTH = D_MODEL // 2
CONV_K = 3
D_FF = 4 * D_MODEL
N_BUCKETS = 32
MAX_DISTANCE = 128
Q_BLOCK = 64
EPS = 1e-6
SPLITS = (ATTN_WIDTH, ATTN_WIDTH, ATTN_WIDTH,
          IDX_HEADS * IDX_DIM, IDX_DIM, IDX_HEADS,
          CONV_WIDTH, CONV_WIDTH, CONV_WIDTH,
          D_MODEL, D_MODEL)
N_IN = sum(SPLITS)

kernel_name = "hybrid_dsa_shortconv_gated_step"

def rmsnorm(x, g):
    xf = x.astype(jnp.float32)
    y = xf * lax.rsqrt(jnp.mean(xf * xf, axis=-1, keepdims=True) + EPS)
    return (y * g.astype(jnp.float32)).astype(x.dtype)

def rel_bucket(n):
    n = jnp.maximum(n, 0)
    max_exact = N_BUCKETS // 2
    nf = jnp.maximum(n, max_exact).astype(jnp.float32)
    large = max_exact + (jnp.log(nf / max_exact) / math.log(MAX_DISTANCE / max_exact)
                         * (N_BUCKETS - max_exact)).astype(jnp.int32)
    large = jnp.minimum(large, N_BUCKETS - 1)
    return jnp.where(n < max_exact, n, large)

def split_proj(h, w_in):
    B, T = h.shape[:2]
    p = h @ w_in
    pieces, off = [], 0
    for w in SPLITS:
        pieces.append(p[..., off:off + w])
        off += w
    q, k, v, qi, ki, wi, cx, cb, cc, ga, gb = pieces
    q = q.reshape(B, T, N_HEADS, HEAD_DIM)
    k = k.reshape(B, T, N_HEADS, HEAD_DIM)
    v = v.reshape(B, T, N_HEADS, HEAD_DIM)
    qi = qi.reshape(B, T, IDX_HEADS, IDX_DIM)
    return q, k, v, qi, ki, wi, cx, cb, cc, ga, gb

def indexer_topk(qi, wi, ki, q_pos, topk):
    s = jnp.einsum('bthd,bsd->bths', qi.astype(jnp.float32), ki.astype(jnp.float32)) * (IDX_DIM ** -0.5)
    score = jnp.einsum('bths,bth->bts', jax.nn.relu(s), wi.astype(jnp.float32) * (IDX_HEADS ** -0.5))
    key_pos = jnp.arange(ki.shape[1])
    adm = key_pos[None, None, :] <= q_pos[None, :, None]
    score = jnp.where(adm, score, -jnp.inf)
    _, idx = lax.top_k(score, topk)
    valid = idx <= q_pos[None, :, None]
    return idx, valid

def sparse_attend(q, k_sel, v_sel, idx, valid, q_pos, rel_bias):
    logits = jnp.einsum('bthd,btkhd->bthk', q.astype(jnp.float32), k_sel.astype(jnp.float32)) * (HEAD_DIM ** -0.5)
    bias = rel_bias.astype(jnp.float32)[rel_bucket(q_pos[None, :, None] - idx)]
    logits = logits + jnp.moveaxis(bias, -1, 2)
    logits = jnp.where(valid[:, :, None, :], logits, -jnp.inf)
    p = jax.nn.softmax(logits, axis=-1)
    out = jnp.einsum('bthk,btkhd->bthd', p, v_sel.astype(jnp.float32))
    return out.astype(q.dtype)

def prompt_attention(q, k, v, qi, ki, wi, rel_bias):
    B, T = q.shape[:2]
    topk = min(TOPK_MAX, T // 4)
    nb = T // Q_BLOCK
    bidx = jnp.arange(B)[:, None, None]

    def block(args):
        qb, qib, wib, pos = args
        idx, valid = indexer_topk(qib, wib, ki, pos, topk)
        ks = k[bidx, idx]
        vs = v[bidx, idx]
        return sparse_attend(qb, ks, vs, idx, valid, pos, rel_bias)

    def to_blocks(a):
        return jnp.moveaxis(a.reshape((B, nb, Q_BLOCK) + a.shape[2:]), 1, 0)

    pos = jnp.arange(T).reshape(nb, Q_BLOCK)
    out = lax.map(block, (to_blocks(q), to_blocks(qi), to_blocks(wi), pos))
    return jnp.moveaxis(out, 0, 1).reshape(B, T, N_HEADS, HEAD_DIM)

def sample_attention(q, k_new, v_new, qi, ki_new, wi, cache_k, cache_v, cache_kidx, page_table, rel_bias):
    DB, T = q.shape[:2]
    n_pages = page_table.shape[1]
    ps = cache_k.shape[1]
    past = n_pages * ps
    topk = min(TOPK_MAX, (past + T) // 4)
    ki_past = cache_kidx[page_table].reshape(DB, past, IDX_DIM)
    ki_all = jnp.concatenate([ki_past.astype(ki_new.dtype), ki_new], axis=1)
    q_pos = past + jnp.arange(T)
    idx, valid = indexer_topk(qi, wi, ki_all, q_pos, topk)
    bidx = jnp.arange(DB)[:, None, None]
    in_past = (idx < past)[..., None, None]
    pidx = jnp.minimum(idx, past - 1)
    phys = page_table[bidx, pidx // ps]
    off = pidx % ps
    nidx = jnp.clip(idx - past, 0, T - 1)
    ks = jnp.where(in_past, cache_k[phys, off].astype(k_new.dtype), k_new[bidx, nidx])
    vs = jnp.where(in_past, cache_v[phys, off].astype(v_new.dtype), v_new[bidx, nidx])
    return sparse_attend(q, ks, vs, idx, valid, q_pos, rel_bias)

def causal_conv(u, prev, conv_w):
    T = u.shape[1]
    full = jnp.concatenate([prev.astype(u.dtype), u], axis=1)
    y = sum(conv_w[j] * full[:, j:j + T] for j in range(CONV_K))
    return y, full[:, -(CONV_K - 1):]

def mix_out(attn, conv_y, cb, ga, gb, w_pa, w_pb, w_o):
    B, T = attn.shape[:2]
    a = attn.reshape(B, T, ATTN_WIDTH) @ w_pa
    c = (cb * conv_y) @ w_pb
    m = jax.nn.sigmoid(ga) * a + jax.nn.sigmoid(gb) * c
    return m @ w_o

def mlp(h, w1, w2):
    return jnp.square(jax.nn.relu(h @ w1)) @ w2

def setup_inputs(seed: int = 0) -> dict:
    key = jax.random.key(seed)
    ks = jax.random.split(key, 20)
    n_pages = PAST_LEN // PAGE_SIZE
    n_pool = (DEC_BATCH * n_pages * 5) // 4
    nrm = lambda k, shape, scale: jax.random.normal(k, shape, jnp.float32) * scale
    page_table = jax.random.permutation(ks[0], n_pool)[:DEC_BATCH * n_pages].reshape(DEC_BATCH, n_pages).astype(jnp.int32)
    return {
        "x_prompt": nrm(ks[1], (BATCH, SEQ, D_MODEL), 1.0),
        "x_sample": nrm(ks[2], (DEC_BATCH, DEC_SEQ, D_MODEL), 1.0),
        "cache_k": nrm(ks[3], (DEPTH, n_pool, PAGE_SIZE, N_HEADS, HEAD_DIM), 1.0),
        "cache_v": nrm(ks[4], (DEPTH, n_pool, PAGE_SIZE, N_HEADS, HEAD_DIM), 1.0),
        "cache_kidx": nrm(ks[5], (DEPTH, n_pool, PAGE_SIZE, IDX_DIM), 1.0),
        "state_conv": nrm(ks[6], (DEPTH, DEC_BATCH, CONV_K - 1, CONV_WIDTH), 1.0),
        "page_table": page_table,
        "rel_bias": nrm(ks[7], (N_BUCKETS, N_HEADS), 0.1),
        "norm_mix_g": 1.0 + nrm(ks[8], (DEPTH, D_MODEL), 0.01),
        "w_in": nrm(ks[9], (DEPTH, D_MODEL, N_IN), D_MODEL ** -0.5),
        "conv_w": nrm(ks[10], (DEPTH, CONV_K, CONV_WIDTH), CONV_K ** -0.5),
        "w_pa": nrm(ks[11], (DEPTH, ATTN_WIDTH, D_MODEL), ATTN_WIDTH ** -0.5),
        "w_pb": nrm(ks[12], (DEPTH, CONV_WIDTH, D_MODEL), CONV_WIDTH ** -0.5),
        "w_o": nrm(ks[13], (DEPTH, D_MODEL, D_MODEL), D_MODEL ** -0.5),
        "norm_mlp_g": 1.0 + nrm(ks[14], (DEPTH, D_MODEL), 0.01),
        "w_mlp_in": nrm(ks[15], (DEPTH, D_MODEL, D_FF), D_MODEL ** -0.5),
        "w_mlp_out": nrm(ks[16], (DEPTH, D_FF, D_MODEL), D_FF ** -0.5),
        "norm_final_g": 1.0 + nrm(ks[17], (D_MODEL,), 0.01),
    }

def reference(x_prompt, x_sample, cache_k, cache_v, cache_kidx, state_conv, page_table, rel_bias,
              norm_mix_g, w_in, conv_w, w_pa, w_pb, w_o, norm_mlp_g, w_mlp_in, w_mlp_out, norm_final_g):
    xp, xs = x_prompt, x_sample
    kp_l, vp_l, kip_l, sp_l, ks_l, vs_l, kis_l, ss_l = [], [], [], [], [], [], [], []
    for l in range(DEPTH):
        hp = rmsnorm(xp, norm_mix_g[l])
        qp, kp, vp, qip, kip, wip, cxp, cbp, ccp, gap, gbp = split_proj(hp, w_in[l])
        ap = prompt_attention(qp, kp, vp, qip, kip, wip, rel_bias)
        up = ccp * cxp
        zero_prev = jnp.zeros((up.shape[0], CONV_K - 1, CONV_WIDTH), up.dtype)
        yconv_p, sp = causal_conv(up, zero_prev, conv_w[l])
        xp = xp + mix_out(ap, yconv_p, cbp, gap, gbp, w_pa[l], w_pb[l], w_o[l])
        xp = xp + mlp(rmsnorm(xp, norm_mlp_g[l]), w_mlp_in[l], w_mlp_out[l])
        hs = rmsnorm(xs, norm_mix_g[l])
        qs, kn, vn, qis, kin, wis, cxs, cbs, ccs, gas, gbs = split_proj(hs, w_in[l])
        a_s = sample_attention(qs, kn, vn, qis, kin, wis, cache_k[l], cache_v[l], cache_kidx[l], page_table, rel_bias)
        us = ccs * cxs
        yconv_s, ss = causal_conv(us, state_conv[l], conv_w[l])
        xs = xs + mix_out(a_s, yconv_s, cbs, gas, gbs, w_pa[l], w_pb[l], w_o[l])
        xs = xs + mlp(rmsnorm(xs, norm_mlp_g[l]), w_mlp_in[l], w_mlp_out[l])
        kp_l.append(kp); vp_l.append(vp); kip_l.append(kip); sp_l.append(sp)
        ks_l.append(kn); vs_l.append(vn); kis_l.append(kin); ss_l.append(ss)
    y_prompt = rmsnorm(xp, norm_final_g)
    y_sample = rmsnorm(xs, norm_final_g)
    k_prompt = jnp.stack(kp_l)
    v_prompt = jnp.stack(vp_l)
    kidx_prompt = jnp.stack(kip_l)
    conv_prompt = jnp.stack(sp_l)
    k_sample = jnp.stack(ks_l)
    v_sample = jnp.stack(vs_l)
    kidx_sample = jnp.stack(kis_l)
    conv_sample = jnp.stack(ss_l)
    return (y_prompt, y_sample, k_prompt, v_prompt, kidx_prompt, conv_prompt,
            k_sample, v_sample, kidx_sample, conv_sample)


_drawn_inputs = setup_inputs


def setup_inputs(seed=0):
    import zlib

    import numpy as np

    out = dict(_drawn_inputs(seed))
    spreads = {}
    factors = {'rel_bias': 42.596,
     'norm_mix_g': 3.937,
     'norm_mlp_g': 37.381,
     'norm_final_g': 31.854,
     'cache_k': 4.249,
     'cache_v': 4.803,
     'cache_kidx': 4.708}
    for name, (base, spread) in spreads.items():
        noise = np.random.default_rng([zlib.crc32(name.encode()), seed]).standard_normal(out[name].shape)
        drawn = base * np.exp(spread * noise) if base else spread * noise
        out[name] = __import__('jax').numpy.asarray(drawn.astype(out[name].dtype))
    for name, factor in factors.items():
        out[name] = (out[name] * factor).astype(out[name].dtype)
    return out
```

```python
from contextlib import ExitStack

import concourse.bass as bass
from concourse import mybir

ALU = mybir.AluOpType
ACT = mybir.ActivationFunctionType
F32 = mybir.dt.float32
I32 = mybir.dt.int32
F32R = mybir.dt.float32r
U32 = mybir.dt.uint32
AX_X = mybir.AxisListType.X

P = 128
D = 2048
KT = D // P
SEQ = 256
DB, DT = 8, 4
NS = DB * DT
TOK = SEQ + NS
H, HD = 8, 128
AW = H * HD
IH, ID = 16, 64
CW = 1024
CT = CW // P
DFF = 4 * D
PAST, PS = 2048, 128
NPG = PAST // PS
POOL = DB * NPG * 5 // 4
TOPK = 256
TOPP = 64
NB = 32
UNITS = TOPK // 4
NEG = -3.0e38
MARK = -3.3e38
CUT = -3.2e38
OFF = -1.0e30
EPS = 1e-6
QKS = float(HD) ** -0.5
BUCKET_LO = list(range(17)) + [19, 21, 24, 27, 31, 35, 40, 46, 52, 59, 67, 77, 87, 99, 113]

CK = 8
CN = 256
RING = 4
TW = 384

Q0, K0, V0, QI0, KI0 = 0, AW, 2 * AW, 3 * AW, 4 * AW
WI0 = KI0 + ID
CX0 = WI0 + IH
CB0, CC0, GA0 = CX0 + CW, CX0 + 2 * CW, CX0 + 3 * CW
GB0 = GA0 + D
NIN = GB0 + D

CONST_P = [("ident", P), ("rs", 4 * P), ("rall", P), ("rnew", P), ("s32", NS), ("b4", P), ("ok4", 4),
           ("iota", NPG), ("tpos", 1), ("nd", DT)]
CONST_E = [("onehot", TW), ("amask", DB * P), ("causal", 3 * P), ("pgsel", P), ("r8", 1)]


def offsets(layout):
    at, out = 0, {}
    for name, n in layout:
        out[name] = (at, n)
        at += n
    return out, at


CP, CPW = offsets(CONST_P)
CE, CEW = offsets(CONST_E)


class Chain:

    def __init__(self, eng, sem):
        self.eng, self.sem, self.n, self.base = eng, sem, 0, None

    def __call__(self, ins):
        ins.then_inc(self.sem, 1)
        self.n += 1
        self.eng.wait_ge(self.sem, self.n if self.base is None else self.base + self.n)

    def enter(self, t, per):
        self.base, self.per, self.n0 = t * per, per, self.n

    def leave(self, times):
        assert self.n - self.n0 == self.per, (self.n - self.n0, self.per)
        self.n = self.n0 + self.per * times
        self.base = None


def build(nc, I, O):
    with ExitStack() as ctx:
        place = {}
        top = [-(-nc.sbuf_base // 64) * 64]

        def sb(name, shape, dt=F32, at=None):
            n = 4
            for d in shape[1:]:
                n *= d
            if at is None:
                at, top[0] = top[0], top[0] + -(-n // 32) * 32
            place[name] = at
            return nc.alloc_sbuf_tensor_at(name, shape, dt, offset=at)

        def view(t, a, shape, parts=P):
            n = 1
            for s in shape:
                n *= s
            v = t[0:parts, a:a + n]
            if len(shape) == 1:
                return v
            names = "abcd"[:len(shape)]
            return v.rearrange(f"p ({' '.join(names)}) -> p {' '.join(names)}", **dict(zip(names, shape)))

        wring = sb("wring", [P, RING, CK, CN])
        xT = sb("xT", [P, KT, TOK])
        hA = sb("hA", [P, KT, TOK])
        zB = sb("zB", [P, KT, TOK])
        G = sb("G", [P, 2 * KT * TOK])
        qT = sb("qT", [P, H, TOK])
        kT = sb("kT", [P, H, TOK])
        uv = sb("uv", [P, CT * (SEQ + 2) + CT * DB * 6])
        kv = sb("kv", [P, 4, AW])
        qrep = sb("qrep", [P, AW])
        knrep = sb("knrep", [P, AW])
        vnrep = sb("vnrep", [P, AW])
        scw = sb("scw", [P, PAST + 4])
        lg = sb("lg", [P, UNITS + 1, H])
        lgt = sb("lgt", [P, 4, H])
        mask2 = sb("mask2", [P, 3 * P])

        cp = sb("cp", [P, CPW])
        m8 = sb("m8", [P, 8])
        m8p = sb("m8p", [P, 8])
        ix = sb("ix", [NS, TOPK], U32)
        comb = sb("comb", [NS, 2 * UNITS + 1, 4])
        offs = sb("offs", [P, UNITS], U32)
        dist = sb("dist", [P, UNITS])
        newsel = sb("newsel", [P, 1])
        small = sb("small", [P, 64])
        rinv = sb("rinv", [P, TOK])
        gcol = sb("gcol", [P, 3 * KT + 3 * CT])
        wiN = sb("wiN", [P, 3, IH])
        kiT = sb("kiT", [P, TOK])
        kiN = sb("kiN", [P, 3, ID])
        sp = sb("sp", [P, 2, H, NS])
        qs2 = sb("qs2", [P, DB, IH, DT])
        var = mask2[:, 0:TOK]
        later = sb("later", [P, P])
        qstep = sb("qstep", [P, 8])
        rb = sb("rb", [NB, H])
        rbr = sb("rbr", [P, NB, H])
        ptf = sb("ptf", [NS, NPG])
        pti = sb("pti", [NS, NPG], I32)
        ptT = sb("ptT", [NPG, DB], I32)
        ptTf = sb("ptTf", [NPG, DB])
        prow = sb("prow", [P, DB], U32)
        ones = sb("ones", [P, P])
        eps = sb("eps", [P, 1])

        XH, XL = sb("XH", [P, KT, TOK], F32R, at=place["qT"]), sb("XL", [P, KT, TOK], F32R, at=place["uv"])
        YH, YL = sb("YH", [P, KT, TOK], F32R, at=place["hA"]), sb("YL", [P, KT, TOK], F32R, at=place["G"] + 4 * KT * TOK)
        WH = sb("WH", [P, 2, CK, CN], F32R, at=place["wring"] + 2 * 4 * CK * CN)
        WL = sb("WL", [P, 2, CK, CN], F32R, at=place["uv"] + 4 * KT * TOK)
        assert place["uv"] + 4 * KT * TOK + 4 * 2 * CK * CN <= place["vnrep"] + 4 * AW

        def flat(t):
            return t[:].rearrange("p a b -> p (a b)")

        zf, kvf, qf, kf = flat(zB), flat(kv), flat(qT), flat(kT)
        sc = scw[0:NS, :]
        btmp = view(scw, 0, [UNITS, H])
        rbd = view(scw, 512, [NB, H])
        pT = scw[:, 768:768 + 3 * P]
        lps = [scw[:, a:a + 3 * P] for a in (1152, 1536)]
        xin, xs = view(G, 0, [2, D]), view(G, 2 * D, [D], NS)
        qiT, ccT = view(G, 0, [H, TOK]), view(G, 0, [CT, TOK])
        biasW = view(G, 2304, [H, SEQ])
        Vp = view(G, 4352, [2, AW])
        Kn, cbT = view(G, 6400, [2, AW]), view(G, 6400, [CT, TOK])
        GA, GB = view(G, 0, [KT, TOK]), view(G, KT * TOK, [KT, TOK])
        ynat, ysam = view(G, KT * TOK, [2, D]), view(zf, 0, [D], NS)
        rawk = ([view(kvf, 1024 * b, [8, P]) for b in range(4)] + [view(G, 6144 + 1024 * b, [8, P]) for b in range(3)]
                + [view(zf, 2048, [8, P])])
        kiP = view(zf, 0, [2, PAST // 2])
        Amat = view(zf, 3072, [DB, P], 2 * NS)
        Wc = view(zf, 4096, [DB, 2 * NS])
        wk = view(qf, 0, [KT, ID + IH])
        ce = kf[:, 0:CEW]
        gN = kf[0:3 * KT + 3 * CT, CEW:CEW + P]
        hN = GA
        tr = view(zf, 0, [2, 2, TOK])
        sq = zB
        stN = kvf[0:2 * DB, 3 * AW:4 * AW]
        table = view(uv, 0, [4, TW])
        rl = view(uv, 0, [2, 512])
        rlp = view(uv, 1024, [2, 3 * P])
        vT = view(uv, 0, [H, TOK])
        up = view(uv, 0, [CT, SEQ + 2])
        us = view(uv, CT * (SEQ + 2), [CT, DB, 6])
        qn, kn, vn = (kv[0:NS, i, :] for i in range(3))
        ulast = view(sp[:].rearrange("p a h n -> p (a h n)"), 0, [CT, 18])
        qswap = view(sp[:].rearrange("p a h n -> p (a h n)"), 0, [H, NS])
        uN = knrep[0:18, :]
        eq, eqp = sc[:, 0:1024].rearrange("p (u g) -> p u g", g=NPG), sc[:, 1024:2048].rearrange("p (u g) -> p u g", g=NPG)
        osb = qrep[0:NS, :]
        smx, smt = lps[0][0:H, 0:P], lps[0][0:H, P:P + NS]

        def const(name, rows=P):
            where, t = (CP, cp) if name in CP else (CE, ce)
            a, n = where[name]
            return t[0:rows, a:a + n]

        PM = ctx.enter_context(nc.psum_tensor("PM", [P, 8, 512], F32))

        S = {n: ctx.enter_context(nc.semaphore(n)) for n in (
            "x_in consts_in early_in wk_in rb_in rbr_in gains_in state_in pt_in qs_moved qs_copied "
            "x_turned x_copied gains_turned gains_copied sq_ready sumsq rms_ready h_ready "
            "kiwi_done kiwi_copied kin_turned kin_copied kin_out amat_ready wc_turned wc_copied "
            "tab_done tab_copied tab_out bias_in consts_set early_free "
            "win_evac chunk_used "
            "pscore_done pscore_relu pscore_acc kp_turned kp_copied sscore_done sscore_relu scomb_done scomb_added "
            "nat_done nat_copied k_out kv_out comb_ready spread_done spread_read pads_zero "
            "plog_done plog_read pmax_ready pexp_done pprob_ready pt_turned pt_copied po_done po_copied "
            "unit_read conv_done tmax_ready tmax_turned tmax_wide tmax_back lg_shifted lg_exp lsum_ready lsum_wide "
            "sp_ready unit_summed o_copied ot_done ot_copied "
            "ul_ready ul_turned ul_copied u_out res_add relu_raw relu_done y_turned y_copied y_out "
            "ptT_in ptT_ready prow_sum prow_ready wh_ready wl_ready xh_ready xl_ready yh_ready yl_ready mix_sum dve_step").split()}
        ld = [ctx.enter_context(nc.semaphore(f"weights_in{i}")) for i in range(RING)]
        ks = [ctx.enter_context(nc.semaphore(f"rows_in{i}")) for i in range(4)]
        pages_in = [ctx.enter_context(nc.semaphore(f"pages_in{i}")) for i in range(DB)]
        tabs = [ctx.enter_context(nc.semaphore(f"table_out{i}")) for i in range(4)]
        scratch = nc.dram_tensor("bias_scratch", [H, P * (TW + 1)], F32, kind="Internal").ap()

        wv = {n: I[n].rearrange("(k p) n -> p k n", p=P) for n in ("w_in", "w_pa", "w_pb", "w_o", "w_mlp_in", "w_mlp_out")}
        SEGS = [QI0, Q0, K0, V0, CX0, CC0, CB0]
        NPAIR = 4 * len(SEGS) + 16
        C_MIX = 2 * NPAIR
        C_WO = C_MIX + 16
        C_MLP = C_WO + 16

        block = ctx.enter_context(nc.Block())

        @block.sync
        def _(eng):
            w = wv["w_in"]

            def half(a, i):
                return a[:, CK * (i % 2):CK * (i % 2) + CK]

            def turn(chunks, used):
                for i, (src, col) in enumerate(chunks):
                    if used is not None:
                        eng.wait_ge(S["chunk_used"], used + i)
                    eng.dma_start(wring[:, i], src[:, :, bass.ds(col, CN)]).then_inc(ld[i], 16)

            def win(col, t):
                return [(half(w, i), t * (2 * CN) + (col + CN * (i // 2))) for i in range(4)]

            eng.dma_start(wk, w[:, :, KI0:KI0 + ID + IH]).then_inc(S["wk_in"], 16)
            turn(win(QI0, 0), None)
            turn(win(QI0, 1), 1)
            for s, col in enumerate(SEGS[1:]):
                with eng.Fori(0, 2) as t:
                    turn(win(col, t), t * 4 + (8 * (s + 1) - RING + 1))
            with eng.Fori(0, 8) as t:
                turn(win(GA0, t), t * 4 + (8 * len(SEGS) - RING + 1))
            def turn2(chunks, split):
                for i, (src, col) in enumerate(chunks):
                    if split is None and i < 2:
                        eng.wait_ge(S["chunk_used"], C_MIX - 3 + i)
                    elif split is None:
                        eng.wait_ge(S["wl_ready"], i - 1)
                    else:
                        eng.wait_ge(S["wl_ready"], split + i)
                    eng.dma_start(wring[:, i % 2], src[:, :, bass.ds(col, CN)]).then_inc(ld[i % 2], 16)

            def mix_chunks(t):
                return [(wv["w_pa" if i % 2 else "w_pb"], t * (2 * CN) + CN * (i // 2)) for i in range(4)]

            turn2(mix_chunks(0), None)
            with eng.Fori(1, 4) as t:
                turn2(mix_chunks(t), t * 4 - 1)
            with eng.Fori(0, 4) as t:
                turn2([(half(wv["w_o"], i), t * (2 * CN) + CN * (i // 2)) for i in range(4)], t * 4 + (C_WO - C_MIX - 1))
            for f in range(DFF // D):
                with eng.Fori(0, 4) as t:
                    turn2([(half(wv["w_mlp_in"], i), t * (2 * CN) + (D * f + CN * (i // 2))) for i in range(4)],
                          t * 4 + (C_MLP - C_MIX + 32 * f - 1))
                with eng.Fori(0, 4) as t:
                    turn2([(half(wv["w_mlp_out"][:, KT * f:KT * f + KT], i), t * (2 * CN) + CN * (i // 2)) for i in range(4)],
                          t * 4 + (C_MLP - C_MIX + 32 * f + 16 - 1))
            for part in range(2):
                eng.wait_ge(S["y_copied"], 4 * (part + 1))
                eng.dma_start(O["y_prompt"][part * P:part * P + P, :], ynat[:, part, :]).then_inc(S["y_out"], 16)
            eng.wait_ge(S["y_copied"], 12)
            eng.dma_start(O["y_sample"], ysam).then_inc(S["y_out"], 16)
            eng.wait_ge(S["y_out"], 48)

        @block.tensor
        def _(pe):
            def bank(i, a=0, n=512, rows=P, r0=0):
                return PM[r0:r0 + rows, i, a:a + n]

            def transpose(out, in_):
                n = in_.shape[0]
                return pe.transpose(out, in_, cp[0:n, 0:n])

            def product(slot, count, b0, rhs, k0, first, last):
                pe.wait_ge(ld[slot], count)
                for o in range(2):
                    for k in range(CK):
                        m = pe.matmul(bank(b0 + o, 0, TOK), wring[:, slot, k, o * P:o * P + P], rhs[:, k0 + k, :],
                                      start=(first and k == 0), stop=(last and k == CK - 1))
                m.then_inc(S["chunk_used"], 1)

            def win_half(p, half):
                if half == 0 and p >= 2:
                    pe.wait_ge(S["win_evac"], p - 1)
                product((2 * p + half) % 4, 16 * ((2 * p + half) // 4 + 1), 2 * (p % 2), hA, CK * half, half == 0, half == 1)

            def win_turns(p0, times, between=None):
                with pe.Fori(0, times) as t:
                    for i in range(4):
                        if i % 2 == 0:
                            pe.wait_ge(S["win_evac"], t * 2 + (p0 + i // 2 - 1))
                        product(i, t * 16 + 16 * (p0 // 2 + 1), 2 * (i // 2), hA, CK * (i % 2), i % 2 == 0, i % 2 == 1)
                        if between:
                            between(t, i)

            def product3(i, split, b0, rhs, k0, first, last):
                pe.wait_ge(S["wl_ready"], split)
                rh, rl_ = rhs
                for o in range(2):
                    for k in range(CK):
                        wh, wl = (w[:, i % 2, k, o * P:o * P + P] for w in (WH, WL))
                        out = bank(b0 + o, 0, TOK)
                        pe.matmul(out, wh, rh[:, k0 + k, :], start=(first and k == 0), stop=False)
                        pe.matmul(out, wh, rl_[:, k0 + k, :], start=False, stop=False)
                        m = pe.matmul(out, wl, rh[:, k0 + k, :], start=False, stop=(last and k == CK - 1))
                m.then_inc(S["chunk_used"], 1)

            def wide(base, rhs, done, n0, before, m0):
                def turn(t, first):
                    for i in range(4):
                        if first:
                            pe.wait_ge(before, m0 - 1 if i == 0 else m0)
                        elif i % 2 == 0:
                            pe.wait_ge(done, t * 2 + (n0 + i // 2 - 1))
                        product3(i, t * 4 + (base - C_MIX + i + 1), 2 * (i // 2), rhs, CK * (i % 2), i % 2 == 0, i % 2 == 1)
                turn(0, True)
                with pe.Fori(1, 4) as t:
                    turn(t, False)

            def sum_squares(n, b):
                for k in range(KT):
                    pe.wait_ge(S["sq_ready"], KT * n + k + 1)
                    m = pe.matmul(bank(b, 0, TOK), ones[:], (sq if n else hA)[:, k, :], start=(k == 0), stop=(k == KT - 1))
                m.then_inc(S["sumsq"], 1)

            pe.wait_ge(S["early_in"], 16)
            pe.wait_ge(S["ptT_ready"], 1)
            pe.matmul(bank(7, 0, DB), const("pgsel", NPG), ptTf[:], start=True, stop=True).then_inc(S["prow_sum"], 1)

            pe.wait_ge(S["consts_in"], 16)
            pe.wait_ge(S["x_in"], 32)
            for k in range(KT):
                if k == 7:
                    pe.wait_ge(S["prow_ready"], 1)
                if k >= 8:
                    pe.wait_ge(S["x_copied"], k - 7)
                for q in range(2):
                    transpose(bank(k % 8, q * P, P), xin[:, q, k * P:k * P + P])
                transpose(bank(k % 8, SEQ, NS), xs[:, k * P:k * P + P]).then_inc(S["x_turned"], 1)
            pe.wait_ge(S["x_copied"], KT)
            pe.wait_ge(S["gains_in"], 64)
            transpose(bank(0, 0, 3 * KT + 3 * CT), gN).then_inc(S["gains_turned"], 1)
            pe.wait_ge(S["consts_set"], 2)
            sum_squares(0, 1)

            pe.wait_ge(S["rb_in"], 16)
            for h in range(H):
                if h >= 2:
                    pe.wait_ge(S["tab_copied"], h - 1)
                pe.matmul(bank(6 + h % 2, 0, TW), rb[:, h:h + 1].to_broadcast([NB, P]), const("onehot", NB),
                          start=True, stop=True).then_inc(S["tab_done"], 1)

            tok_tiles = ((0, P), (P, P), (SEQ, NS))
            pe.wait_ge(S["wk_in"], 16)
            pe.wait_ge(S["h_ready"], KT)
            for half in range(2):
                for k in range(KT):
                    pe.matmul(bank(2, 0, TOK, ID, ID * half), wk[:, k, 0:ID], hA[:, k, :], start=(k == 0), stop=(k == KT - 1))
            for j, (a, n, r0) in enumerate(((0, P, 0), (P, P, 0), (SEQ, NS, 0), (SEQ, NS, NS))):
                for k in range(KT):
                    m = pe.matmul(bank(3, IH * min(j, 2), IH, n, r0), hA[:, k, a:a + n], wk[:, k, ID:ID + IH],
                                  start=(k == 0), stop=(k == KT - 1))
            m.then_inc(S["kiwi_done"], 1)
            pe.wait_ge(S["kiwi_copied"], 3)
            for j, (a, n) in enumerate(tok_tiles):
                m = transpose(bank(4, ID * j, ID, n), kiT[0:ID, a:a + n])
            m.then_inc(S["kin_turned"], 1)
            pe.wait_ge(S["amat_ready"], 1)
            for j in range(DB):
                m = transpose(bank(5, 2 * NS * j, 2 * NS), Amat[:, j, :])
            m.then_inc(S["wc_turned"], 1)

            for p in range(4):
                win_half(p, 0)
                win_half(p, 1)

            pe.wait_ge(S["win_evac"], 4)
            pe.wait_ge(S["tab_copied"], H)
            pe.wait_ge(S["wc_copied"], 1)
            for h in range(IH):
                r, j = ID * (h % 2), h // 2
                if h >= 4:
                    pe.wait_ge(S["pscore_relu"], h - 3)
                pe.matmul(bank(4 + h % 4, 0, P), qiT[r:r + ID, j, 0:P], kiT[r:r + ID, 0:P], start=True, stop=True)
                pe.matmul(bank(4 + h % 4, P, SEQ), qiT[r:r + ID, j, P:SEQ], kiT[r:r + ID, 0:SEQ],
                          start=True, stop=True).then_inc(S["pscore_done"], 1)

            pe.wait_ge(S["qs_copied"], 4)
            pe.wait_ge(S["pscore_relu"], IH)

            def turn_keys(b):
                pe.wait_ge(pages_in[b], 16)
                for c in range(2):
                    at = 2 * b + c
                    if at >= 3:
                        pe.wait_ge(S["kp_copied"], at - 2)
                    for g in range(4):
                        m = transpose(bank(4 + at % 3, g * P, P), rawk[b][:, 4 * c + g, :])
                    m.then_inc(S["kp_turned"], 1)

            def scores(b, c):
                at = 3 * b + c
                if at >= 2:
                    pe.wait_ge(S["sscore_relu"], at - 1)
                if c < 2:
                    pe.wait_ge(S["kp_copied"], 2 * b + 2)
                for e in range(2 if c < 2 else 1):
                    r = ID * e
                    rhs = kiP[r:r + ID, b % 2, 512 * c:512 * c + 512] if c < 2 else kiT[0:ID, SEQ + DT * b:SEQ + DT * b + DT]
                    m = pe.matmul(PM[r:r + ID, at % 2, 0:rhs.shape[1]], qs2[r:r + ID, b].rearrange("p h t -> p (h t)"), rhs,
                                  start=True, stop=True)
                m.then_inc(S["sscore_done"], 1)

            def combine(b, c):
                at = 3 * b + c
                pe.wait_ge(S["sscore_relu"], at + 1)
                if c < 2:
                    m = pe.matmul(bank(2 + c, 0, 512, 2 * NS), Wc[:, b, :], rl[:, at % 2, :], start=(b == 0), stop=(b == DB - 1))
                else:
                    m = pe.matmul(bank(7, 0, DT, NS), Wc[0:ID, b, 0:NS], rl[0:ID, at % 2, 0:DT], start=(b == 0), stop=(b == DB - 1))
                m.then_inc(S["scomb_done"], 1)

            turn_keys(0)
            for b in range(DB):
                if b + 1 < DB:
                    turn_keys(b + 1)
                scores(b, 0)
                scores(b, 1)
                combine(b, 0)
                scores(b, 2)
                combine(b, 1)
                combine(b, 2)
            pe.wait_ge(S["scomb_added"], 5)

            win_turns(4, 6)

            pe.wait_ge(S["win_evac"], 16)
            nat = [0]

            def next_bank():
                if nat[0] >= 4:
                    pe.wait_ge(S["nat_copied"], nat[0] - 3)
                nat[0] += 1
                return 4 + (nat[0] - 1) % 4

            for src in (vT, kT):
                for q in range(2):
                    for quad in range(2):
                        b = next_bank()
                        for i in range(4):
                            m = transpose(bank(b, i * P, P), src[:, 4 * quad + i, q * P:q * P + P])
                        m.then_inc(S["nat_done"], 1)
            for src in (qT, kT, vT):
                for quad in range(2):
                    b = next_bank()
                    for i in range(4):
                        m = transpose(bank(b, i * P, P, NS), src[:, 4 * quad + i, SEQ:TOK])
                    m.then_inc(S["nat_done"], 1)
            for j, (src, pick) in enumerate(((qn, "rall"), (kn, "rnew"), (vn, "rnew"))):
                pe.wait_ge(S["nat_copied"], 10 + 2 * j)
                for half in range(2):
                    b = next_bank()
                    pe.matmul(bank(b), const(pick, NS), src[:, 512 * half:512 * half + 512],
                              start=True, stop=True).then_inc(S["nat_done"], 1)
            pe.wait_ge(S["state_in"], 16)
            b = next_bank()
            for i in range(CT):
                m = transpose(bank(b, 2 * DB * i, 2 * DB), stN[:, i * P:i * P + P])
            m.then_inc(S["nat_done"], 1)

            for p in (16, 17):
                win_half(p, 0)
                win_half(p, 1)
            pe.wait_ge(S["comb_ready"], 1)
            pe.wait_ge(S["nat_copied"], 21)
            for s in range(4):
                m = pe.matmul(bank(7, 0, 2 * UNITS + 1), const("rs", NS)[:, s * P:s * P + P], comb[:, :, s],
                              start=(s == 0), stop=(s == 3))
            m.then_inc(S["spread_done"], 1)
            for p in (18, 19):
                win_half(p, 0)
                win_half(p, 1)

            def prompt_logits(h):
                if h:
                    pe.wait_ge(S["plog_read"], h)
                pe.matmul(bank(4, 0, P), qT[:, h, 0:P], kT[:, h, 0:P], start=True, stop=True)
                pe.matmul(bank(4, P, SEQ), qT[:, h, P:SEQ], kT[:, h, 0:SEQ], start=True, stop=True).then_inc(S["plog_done"], 1)

            def prompt_turn(h):
                pe.wait_ge(S["pprob_ready"], h + 1)
                if h:
                    pe.wait_ge(S["pt_copied"], h)
                for i in range(3):
                    m = transpose(bank(5, i * P, P), lps[h % 2][:, i * P:i * P + P])
                m.then_inc(S["pt_turned"], 1)

            def prompt_out(h):
                pe.wait_ge(S["pt_copied"], h + 1)
                if h:
                    pe.wait_ge(S["po_copied"], h)
                pe.matmul(bank(6, 0, SEQ), Vp[:, 0, h * HD:h * HD + HD], pT[:, 0:SEQ], start=True, stop=False)
                pe.matmul(bank(6, P, P), Vp[:, 1, h * HD:h * HD + HD], pT[:, SEQ:3 * P], start=False, stop=True).then_inc(S["po_done"], 1)

            for j in range(H):
                prompt_logits(j)
                win_half(20 + j, 0)
                if j:
                    prompt_turn(j - 1)
                win_half(20 + j, 1)
                if j:
                    prompt_out(j - 1)
            prompt_turn(H - 1)
            prompt_out(H - 1)

            win_turns(28, 4)

            pe.wait_ge(S["ul_ready"], 1)
            pe.wait_ge(S["po_copied"], H)
            for half in range(2):
                for i in range(4):
                    m = transpose(bank(5 + half, i * P, P, 18), ulast[:, 4 * half + i, :])
                m.then_inc(S["ul_turned"], 1)
            pe.wait_ge(S["tmax_ready"], 1)
            transpose(bank(4, 0, P, H), small[:, 0:H]).then_inc(S["tmax_turned"], 1)
            pe.wait_ge(S["tmax_wide"], 1)
            transpose(bank(7, 0, H), smx).then_inc(S["tmax_back"], 1)
            pe.wait_ge(S["lsum_ready"], 1)
            pe.matmul(bank(4, 0, H), const("b4"), small[:, 16:16 + H], start=True, stop=True).then_inc(S["lsum_wide"], 1)
            pe.wait_ge(S["ul_copied"], 2)

            def unit_sum(ring, rows, first=False):
                for h in range(H):
                    m = pe.matmul(PM[0:NS, 6 + h // 4, (h % 4) * HD:(h % 4) * HD + HD], sp[:, ring, h, :], rows[:, h * HD:h * HD + HD],
                                  start=(first and h % 4 == 0), stop=False, skip_group_check=True)
                m.then_inc(S["unit_summed"], 1)

            def v_units(t, i):
                for r in range(4):
                    pe.wait_ge(S["sp_ready"], t * 16 + (4 * i + r + 2))
                    pe.wait_ge(ks[r], t * 64 + 16 * (UNITS // 4 + i + 1))
                    unit_sum((1 + r) % 2, kv[:, r, :])

            pe.wait_ge(S["sp_ready"], 1)
            unit_sum(0, vnrep[:], True)
            win_turns(36, 4, v_units)
            pe.wait_ge(S["o_copied"], 1)
            for i in range(H):
                m = transpose(bank(4, i * NS, NS), osb[:, i * P:i * P + P])
            m.then_inc(S["ot_done"], 1)
            pe.wait_ge(S["ot_copied"], 1)

            pe.wait_ge(S["win_evac"], NPAIR)

            def mix_turn(t, first):
                for i in range(4):
                    if first and i < 2:
                        pe.wait_ge(S["xl_ready"], i + 1)
                    elif not first and i % 2 == 0:
                        pe.wait_ge(S["yl_ready"], t * 2 + (i // 2 - 1))
                    product3(i, t * 4 + (i + 1), 4 * (i // 2) + 2 * (i % 2), (XH, XL), CT * (i % 2), True, True)

            mix_turn(0, True)
            with pe.Fori(1, 4) as t:
                mix_turn(t, False)

            wide(C_WO, (YH, YL), S["res_add"], 0, S["yl_ready"], 8)
            sum_squares(1, 4)
            pe.wait_ge(S["xl_ready"], 2 + KT // 2)
            for f in range(DFF // D):
                wide(C_MLP + 32 * f, (XH, XL), S["yl_ready"], 8 * (f + 1), S["res_add"], 8 * (f + 1))
                wide(C_MLP + 32 * f + 16, (YH, YL), S["res_add"], 8 * (f + 1), S["yl_ready"], 8 * (f + 2))
            sum_squares(2, 4)
            pe.wait_ge(S["h_ready"], 3 * KT)
            n = 0
            for a, rows in tok_tiles:
                for quad in range(4):
                    if n >= 4:
                        pe.wait_ge(S["y_copied"], n - 3)
                    for i in range(4):
                        m = transpose(bank(n % 4, i * P, P, rows), hN[:, 4 * quad + i, a:a + rows])
                    m.then_inc(S["y_turned"], 1)
                    n += 1

        @block.scalar
        def _(act):
            def bank(i, a=0, n=512, rows=P, r0=0):
                return PM[r0:r0 + rows, i, a:a + n]

            def copy(out, in_, **kw):
                return act.activation(out, in_, ACT.Copy, **kw)

            with nc.allow_non_contiguous_dma(reason="128 page numbers, turned"):
                act.dma_start(ptT[:], I["page_table"].rearrange("b g -> g b")).then_inc(S["ptT_in"], 16)
            act.dma_start(ce, I["const_e"]).then_inc(S["early_in"], 16)
            act.dma_start(cp[:], I["const_p"]).then_inc(S["consts_in"], 16)
            act.dma_start(xin, I["x_prompt"].rearrange("(q p) d -> p q d", p=P)).then_inc(S["x_in"], 16)
            act.dma_start(xs, I["x_sample"]).then_inc(S["x_in"], 16)
            for i, (name, n) in enumerate((("norm_mix_g", KT), ("norm_mlp_g", KT), ("norm_final_g", KT), ("conv_w", 3 * CT))):
                act.dma_start(gN[KT * i:KT * i + n, :], I[name].rearrange("a (i p) -> (a i) p", p=P)).then_inc(S["gains_in"], 16)
            act.dma_start(rb[:], I["rel_bias"]).then_inc(S["rb_in"], 16)
            act.dma_start(rbr[:].rearrange("p a b -> p (a b)"),
                          I["rel_bias"].rearrange("(o a) b -> o (a b)", o=1).to_broadcast([P, NB * H])).then_inc(S["rbr_in"], 16)
            for t in range(DT):
                act.dma_start(pti[t:NS:DT, :], I["page_table"]).then_inc(S["pt_in"], 16)

            def squares(n, wait):
                for k in range(KT):
                    if wait:
                        act.wait_ge(S["x_copied"], k + 1)
                    act.activation((sq if n else hA)[:, k, :], xT[:, k, :], ACT.Square).then_inc(S["sq_ready"], 1)

            def root(n, b):
                act.wait_ge(S["sumsq"], n + 1)
                if n:
                    act.wait_ge(S["h_ready"], KT * n)
                act.activation(rinv[:], bank(b, 0, TOK), ACT.Sqrt, bias=eps[:, 0:1], scale=1.0 / D).then_inc(S["rms_ready"], 1)

            squares(0, True)
            act.wait_ge(S["gains_turned"], 1)
            copy(gcol[:], bank(0, 0, 3 * KT + 3 * CT)).then_inc(S["gains_copied"], 1)
            act.wait_ge(S["consts_set"], 2)
            root(0, 1)

            for h in range(H):
                act.wait_ge(S["tab_done"], h + 1)
                if h >= 4:
                    act.wait_ge(tabs[h % 4], 16)
                copy(table[:, h % 4, :], bank(6 + h % 2, 0, TW)).then_inc(S["tab_copied"], 1)
                act.wait_ge(S["tab_copied"], h + 1)
                act.dma_start(scratch[h].rearrange("(p w) -> p w", w=TW + 1)[:, 0:TW], table[:, h % 4, :]).then_inc(tabs[h % 4], 16)
            for i in range(4):
                act.wait_ge(tabs[i], 32)
            act.dma_start(biasW, scratch[:, 0:P * TW].rearrange("h (p w) -> p h w", w=TW)[:, :, P - 1:P - 1 + SEQ]).then_inc(S["bias_in"], 16)

            act.wait_ge(S["kiwi_done"], 1)
            copy(kiT[:], bank(2, 0, TOK)).then_inc(S["kiwi_copied"], 1)
            wis = float(ID) ** -0.5 * float(IH) ** -0.5
            copy(wiN[:, 0:2, :], bank(3, 0, 2 * IH), scale=wis).then_inc(S["kiwi_copied"], 1)
            copy(wiN[0:2 * NS, 2, :], bank(3, 2 * IH, IH, 2 * NS), scale=wis).then_inc(S["kiwi_copied"], 1)
            act.wait_ge(S["kin_turned"], 1)
            copy(kiN[:, 0:2, :], bank(4, 0, 2 * ID)).then_inc(S["kin_copied"], 1)
            copy(kiN[0:NS, 2, :], bank(4, 2 * ID, ID, NS)).then_inc(S["kin_copied"], 1)
            act.wait_ge(S["kin_copied"], 2)
            act.dma_start(O["kidx_prompt"].rearrange("(q p) d -> p q d", p=P), kiN[:, 0:2, :]).then_inc(S["kin_out"], 16)
            act.dma_start(O["kidx_sample"], kiN[0:NS, 2, :]).then_inc(S["kin_out"], 16)
            act.wait_ge(S["wc_turned"], 1)
            copy(Wc.rearrange("p a b -> p (a b)"), bank(5, 0, 2 * DB * NS)).then_inc(S["wc_copied"], 1)

            def evac(p, out, func=ACT.Copy):
                act.wait_ge(S["chunk_used"], 2 * p + 2)
                act.activation(out, PM[:, 2 * (p % 2):2 * (p % 2) + 2, 0:TOK], func).then_inc(S["win_evac"], 1)

            for p in range(4):
                evac(p, qiT[:, 2 * p:2 * p + 2, :])
            act.wait_ge(S["win_evac"], 4)
            act.dma_start(qswap[0:ID], qiT[ID:P, :, SEQ:TOK]).then_inc(S["qs_moved"], 16)
            act.dma_start(qswap[ID:P], qiT[0:ID, :, SEQ:TOK]).then_inc(S["qs_moved"], 16)
            by = qs2[:].rearrange("p b (j e) t -> p e j b t", e=2)
            own = qiT[:, :, SEQ:TOK].rearrange("p j (b t) -> p j b t", b=DB)
            swapped = qswap.rearrange("p j (b t) -> p j b t", b=DB)
            for half, e, src in ((0, 0, own), (1, 1, own), (0, 1, swapped), (1, 0, swapped)):
                if src is swapped:
                    act.wait_ge(S["qs_moved"], 32)
                for j in range(H):
                    m = copy(by[ID * half:ID * half + ID, e, j], src[ID * half:ID * half + ID, j])
                m.then_inc(S["qs_copied"], 1)

            for h in range(IH):
                act.wait_ge(S["pscore_done"], h + 1)
                if h >= 2:
                    act.wait_ge(S["pscore_acc"], h - 1)
                act.activation(rlp[:, h % 2, :], bank(4 + h % 4, 0, 3 * P), ACT.Relu).then_inc(S["pscore_relu"], 1)
            for at in range(3 * DB):
                n, rows = (512, P) if at % 3 < 2 else (DT, ID)
                act.wait_ge(S["sscore_done"], at + 1)
                if at >= 2:
                    act.wait_ge(S["scomb_done"], at - 1)
                act.activation(rl[0:rows, at % 2, 0:n], bank(at % 2, 0, n, rows), ACT.Relu).then_inc(S["sscore_relu"], 1)
            act.wait_ge(S["kp_turned"], 16)
            act.dma_start(stN, I["state_conv"]).then_inc(S["state_in"], 16)

            for p in range(4, 8):
                evac(p, qT[:, 2 * (p - 4):2 * (p - 4) + 2, :])
            act.wait_ge(S["early_free"], 1)
            for p in range(8, 12):
                evac(p, kT[:, 2 * (p - 8):2 * (p - 8) + 2, :])
            act.wait_ge(S["pscore_acc"], IH)
            for p in range(12, 16):
                evac(p, vT[:, 2 * (p - 12):2 * (p - 12) + 2, :])

            def nat(n, out, in_):
                act.wait_ge(S["nat_done"], n + 1)
                copy(out, in_).then_inc(S["nat_copied"], 1)

            n = 0
            for dst in (Vp, Kn):
                for q in range(2):
                    for quad in range(2):
                        nat(n, dst[:, q, 512 * quad:512 * quad + 512], bank(4 + n % 4))
                        n += 1
            for dst in (qn, kn, vn):
                for quad in range(2):
                    nat(n, dst[:, 512 * quad:512 * quad + 512], bank(4 + n % 4, rows=NS))
                    n += 1
            for dst in (qrep, knrep, vnrep):
                for half in range(2):
                    nat(n, dst[:, 512 * half:512 * half + 512], bank(4 + n % 4))
                    n += 1
            nat(n, us[:, :, :, 0:2], bank(4 + n % 4, 0, 2 * CT * DB).rearrange("p (i b j) -> p i b j", i=CT, b=DB))
            act.wait_ge(S["nat_copied"], n + 1)
            act.dma_start(O["k_prompt"].rearrange("(q p) d -> p q d", p=P), Kn).then_inc(S["k_out"], 16)
            act.dma_start(O["v_prompt"].rearrange("(q p) d -> p q d", p=P), Vp).then_inc(S["k_out"], 16)
            act.dma_start(O["k_sample"], kn).then_inc(S["kv_out"], 16)
            act.dma_start(O["v_sample"], vn).then_inc(S["kv_out"], 16)

            for p in range(16, 20):
                evac(p, zB[:, CT + 2 * (p - 16):CT + 2 * (p - 16) + 2, :])

            def prompt_turned(h):
                act.wait_ge(S["pt_turned"], h + 1)
                if h:
                    act.wait_ge(S["po_done"], h)
                copy(pT[:], bank(5, 0, 3 * P)).then_inc(S["pt_copied"], 1)

            def prompt_copied(h):
                act.wait_ge(S["po_done"], h + 1)
                copy(zB[:, h, 0:SEQ], bank(6, 0, SEQ)).then_inc(S["po_copied"], 1)

            for j in range(H):
                if j:
                    prompt_turned(j - 1)
                act.wait_ge(S["pmax_ready"], j + 1)
                for i, (a, b) in enumerate(((0, P), (P, 3 * P))):
                    act.activation(lps[j % 2][:, a:b], lps[j % 2][:, a:b], ACT.Exp, bias=qstep[:, i:i + 1],
                                   accum_out=qstep[:, 2 + i:3 + i]).then_inc(S["pexp_done"], 1)
                if j == 4:
                    act.wait_ge(S["k_out"], 32)
                evac(20 + j, (ccT if j < 4 else cbT)[:, 2 * (j % 4):2 * (j % 4) + 2, :])
                if j:
                    prompt_copied(j - 1)
            prompt_turned(H - 1)
            prompt_copied(H - 1)

            act.wait_ge(S["conv_done"], 1)
            for p in range(28, 36):
                evac(p, GA[:, 2 * (p - 28):2 * (p - 28) + 2, :], ACT.Sigmoid)
            for half in range(2):
                act.wait_ge(S["ul_turned"], half + 1)
                if half == 0:
                    act.wait_ge(S["tmax_ready"], 1)
                copy(uN[:, 512 * half:512 * half + 512], bank(5 + half, rows=18)).then_inc(S["ul_copied"], 1)
            act.wait_ge(S["ul_copied"], 2)
            act.dma_start(O["conv_prompt"], uN[0:2, :]).then_inc(S["u_out"], 16)
            act.dma_start(O["conv_sample"], uN[2:18, :]).then_inc(S["u_out"], 16)
            act.wait_ge(S["lg_shifted"], 1)
            act.activation(lg[:], lg[:], ACT.Exp).then_inc(S["lg_exp"], 1)
            act.activation(XH[:, 0:CT, :], zB[:, CT:KT, :], ACT.Copy).then_inc(S["xh_ready"], 1)
            for p in range(36, 44):
                evac(p, GB[:, 2 * (p - 36):2 * (p - 36) + 2, :], ACT.Sigmoid)

            def high(c):
                n = c - C_MIX
                act.wait_ge(ld[n % 2], 16 * (C_MIX // 4 + n // 2 + 1))
                act.wait_ge(S["chunk_used"], c - 1)
                copy(WH[:, n % 2], wring[:, n % 2]).then_inc(S["wh_ready"], 1)

            def high_pair(c):
                if c < C_MLP + 32 * (DFF // D):
                    high(c)
                    high(c + 1)

            act.wait_ge(S["chunk_used"], C_MIX)
            high_pair(C_MIX)
            act.wait_ge(S["unit_summed"], UNITS + 1)
            copy(osb.rearrange("p (a b) -> p a b", a=2), PM[0:NS, 6:8, :]).then_inc(S["o_copied"], 1)
            act.wait_ge(S["ot_done"], 1)
            copy(zB[:, 0:H, SEQ:TOK], bank(4, 0, H * NS).rearrange("p (h n) -> p h n", h=H)).then_inc(S["ot_copied"], 1)
            act.wait_ge(S["ot_copied"], 1)
            act.activation(XH[:, CT:KT, :], zB[:, 0:H, :], ACT.Copy).then_inc(S["xh_ready"], 1)
            for n in range(8):
                high_pair(C_MIX + 2 * n + 2)
                act.wait_ge(S["mix_sum"], n + 1)
                copy(YH[:, 2 * n:2 * n + 2, :], GA[:, 2 * n:2 * n + 2, :]).then_inc(S["yh_ready"], 1)
            for w in range(8):
                high_pair(C_WO + 2 * w + 2)
            act.wait_ge(S["res_add"], 8)
            squares(1, False)
            root(1, 4)
            for k in range(0, KT, 2):
                act.wait_ge(S["h_ready"], KT + k + 2)
                copy(XH[:, k:k + 2, :], hN[:, k:k + 2, :]).then_inc(S["xh_ready"], 1)
            for f in range(DFF // D):
                for w in range(8):
                    n = 8 * f + w
                    high_pair(C_MLP + 32 * f + 2 * w + 2)
                    act.wait_ge(S["chunk_used"], C_MLP + 32 * f + 2 * w + 2)
                    if n >= 2:
                        act.wait_ge(S["yl_ready"], 8 + n - 1)
                    act.activation(tr[:, w % 2], PM[:, 2 * (w % 2):2 * (w % 2) + 2, 0:TOK], ACT.Relu).then_inc(S["relu_raw"], 1)
                    act.wait_ge(S["relu_raw"], n + 1)
                    act.activation(YH[:, 2 * w:2 * w + 2, :], tr[:, w % 2], ACT.Square).then_inc(S["yh_ready"], 1)
                for w in range(8):
                    high_pair(C_MLP + 32 * f + 16 + 2 * w + 2)
            act.wait_ge(S["res_add"], 40)
            squares(2, False)
            root(2, 4)
            act.wait_ge(S["kin_out"], 32)
            act.wait_ge(S["kv_out"], 32)

        @block.vector
        def _(dve):
            step = Chain(dve, S["dve_step"])

            def bank(i, a=0, n=512, rows=P, r0=0):
                return PM[r0:r0 + rows, i, a:a + n]

            dve.memset(ones[:], 1.0).then_inc(S["consts_set"], 1)
            dve.memset(eps[:], EPS).then_inc(S["consts_set"], 1)
            dve.wait_ge(S["ptT_in"], 16)
            dve.tensor_copy(ptTf[:], ptT[:]).then_inc(S["ptT_ready"], 1)
            dve.wait_ge(S["early_in"], 16)
            dve.wait_ge(S["prow_sum"], 1)
            dve.tensor_scalar(prow[:], bank(7, 0, DB), 8.0, const("r8")[:, 0:1], ALU.mult, ALU.add).then_inc(S["prow_ready"], 1)
            for k in range(KT):
                dve.wait_ge(S["x_turned"], k + 1)
                dve.tensor_copy(xT[:, k, :], bank(k % 8, 0, TOK)).then_inc(S["x_copied"], 1)

            def normalise(n):
                dve.wait_ge(S["rms_ready"], n + 1)
                step(dve.tensor_scalar(var, bank(1 if n == 0 else 4, 0, TOK), -0.5 / D, -0.5 * EPS, ALU.mult, ALU.add))
                step(dve.reciprocal(rinv[:], rinv[:]))
                step(dve.tensor_tensor(var, var, rinv[:], ALU.mult))
                step(dve.tensor_tensor(var, var, rinv[:], ALU.mult))
                step(dve.scalar_tensor_tensor(out=rinv[:], in0=var, scalar=1.5, in1=rinv[:], op0=ALU.add, op1=ALU.mult))
                if n == 0:
                    dve.wait_ge(S["gains_copied"], 1)
                for k in range(KT):
                    dve.scalar_tensor_tensor(out=(hN if n else hA)[:, k, :], in0=xT[:, k, :], scalar=gcol[:, KT * n + k:KT * n + k + 1],
                                             in1=rinv[:], op0=ALU.mult, op1=ALU.mult).then_inc(S["h_ready"], 1)

            dve.wait_ge(S["x_copied"], KT)
            normalise(0)

            dve.wait_ge(S["h_ready"], KT)
            step(dve.memset(mask2[:], 0.0))

            dve.wait_ge(S["early_in"], 16)
            dve.wait_ge(S["kiwi_copied"], 3)
            for j in range(DB):
                m = dve.tensor_tensor(Amat[:, j, :].rearrange("p (b h t) -> p b h t", b=2, h=IH),
                                      const("amask", 2 * NS)[:, P * j:P * j + P].rearrange("p (b h t) -> p b h t", b=2, h=IH),
                                      wiN[0:2 * NS, 2, :].unsqueeze(1).unsqueeze(3).to_broadcast([2 * NS, 2, IH, DT]), ALU.mult)
            m.then_inc(S["amat_ready"], 1)
            dve.wait_ge(S["pt_in"], 16 * DT)
            dve.tensor_copy(ptf[:], pti[:])

            for h in range(IH):
                dve.wait_ge(S["pscore_relu"], h + 1)
                if h:
                    dve.wait_ge(S["pscore_acc"], h)
                for q, (a, b) in enumerate(((0, P), (P, 3 * P))):
                    m = dve.scalar_tensor_tensor(out=mask2[:, a:b], in0=rlp[:, h % 2, a:b], scalar=wiN[:, q, h:h + 1],
                                                 in1=mask2[:, a:b], op0=ALU.mult, op1=ALU.add)
                m.then_inc(S["pscore_acc"], 1)
            dve.wait_ge(S["pscore_acc"], IH)
            step(dve.tensor_scalar(lps[0][:], const("causal"), -1.0, -NEG, ALU.add, ALU.mult))
            step(dve.tensor_scalar(later[:], const("causal")[:, 0:P], -1.0, -OFF, ALU.add, ALU.mult))
            step(dve.tensor_tensor(mask2[:], mask2[:], const("causal"), ALU.mult))
            dve.tensor_tensor(mask2[:], mask2[:], lps[0][:], ALU.add).then_inc(S["early_free"], 1)

            for at in range(2 * DB):
                b, c = at // 2, at % 2
                dve.wait_ge(S["kp_turned"], at + 1)
                if b >= 2:
                    dve.wait_ge(S["sscore_done"], 3 * (b - 1))
                dve.tensor_copy(kiP[:, b % 2, :].rearrange("x (p j) -> x p j", j=8)[:, :, 4 * c:4 * c + 4],
                                bank(4 + at % 3).rearrange("x (j p) -> x p j", j=4)).then_inc(S["kp_copied"], 1)
            dve.wait_ge(S["scomb_done"], 3 * DB)
            for c in range(2):
                for e in range(2):
                    dve.tensor_copy(sc[:, 1024 * c:1024 * c + 1024].rearrange("n (m e) -> n m e", e=2)[:, :, e],
                                    PM[NS * e:NS * e + NS, 2 + c, :]).then_inc(S["scomb_added"], 1)
            dve.tensor_copy(sc[:, PAST:], bank(7, 0, DT, NS)).then_inc(S["scomb_added"], 1)
            dve.wait_ge(S["scomb_added"], 5)
            step(dve.tensor_tensor(sc[:, PAST:], sc[:, PAST:], const("ok4", NS), ALU.mult))
            step(dve.tensor_scalar(m8[0:NS, 0:4], const("ok4", NS), -1.0, -NEG, ALU.add, ALU.mult))
            step(dve.tensor_tensor(sc[:, PAST:], sc[:, PAST:], m8[0:NS, 0:4], ALU.add))

            for i in range(TOPK // 8):
                step(dve.max(m8[0:NS, :], sc[:]))
                step(dve.max_index(ix[:, 8 * i:8 * i + 8], m8[0:NS, :], sc[:]))
                step(dve.match_replace(sc[:], m8[0:NS, :], sc[:], MARK))
            step(dve.tensor_scalar(comb[:, 2 * UNITS, :], sc[:, PAST:], CUT, None, ALU.is_le))
            pos = comb[:, UNITS:2 * UNITS, :].rearrange("p u s -> p (u s)")
            rows = comb[:, 0:UNITS, :].rearrange("p u s -> p (u s)")
            step(dve.tensor_copy(pos, ix[:]))
            step(dve.tensor_scalar(ix[:], ix[:], float(PAST - 1), None, ALU.min))
            step(dve.tensor_copy(rows, ix[:]))
            step(dve.tensor_scalar(ix[:], ix[:], 7, None, ALU.logical_shift_right))
            for a in range(0, TOPK, 64):
                step(dve.tensor_tensor(eq, ix[:, a:a + 64].unsqueeze(2).to_broadcast([NS, 64, NPG]),
                                       const("iota", NS).unsqueeze(1).to_broadcast([NS, 64, NPG]), ALU.is_equal))
                step(dve.tensor_tensor(eqp, eq, ptf[:].unsqueeze(1).to_broadcast([NS, 64, NPG]), ALU.mult))
                step(dve.tensor_reduce(eq[:, 0:4, :].rearrange("p u g -> p (u g)"), eqp, AX_X, ALU.add))
                flat_eq = eq[:, 0:4, :].rearrange("p u g -> p (u g)")
                step(dve.tensor_tensor(flat_eq, flat_eq, ix[:, a:a + 64], ALU.subtract))
                m = dve.scalar_tensor_tensor(out=rows[:, a:a + 64], in0=flat_eq, scalar=float(PS), in1=rows[:, a:a + 64],
                                             op0=ALU.mult, op1=ALU.add)
                if a + 64 < TOPK:
                    step(m)
            m.then_inc(S["comb_ready"], 1)

            for a, b in ((0, P), (P, 3 * P)):
                for i in range(TOPP // 8):
                    step(dve.max(m8p[:], mask2[:, a:b]))
                    step(dve.match_replace(mask2[:, a:b], m8p[:], mask2[:, a:b], MARK))
            step(dve.tensor_scalar(mask2[:], mask2[:], CUT, OFF, ALU.is_gt, ALU.mult))
            for a in (0, 2 * P):
                step(dve.tensor_tensor(mask2[:, a:a + P], mask2[:, a:a + P], later[:], ALU.add))

            dve.wait_ge(S["spread_done"], 1)
            dve.tensor_copy(offs[:], bank(7, 0, UNITS))
            dve.tensor_scalar(dist[:], bank(7, UNITS, UNITS), -1.0, const("tpos")[:, 0:1], ALU.mult, ALU.add)
            dve.tensor_copy(newsel[:], bank(7, 2 * UNITS, 1))
            ge = small[:, 0:UNITS]
            dve.tensor_scalar(ge, bank(7, UNITS, UNITS), PAST - 0.5, OFF, ALU.is_gt, ALU.mult).then_inc(S["spread_read"], 1)
            dve.wait_ge(S["spread_read"], 1)
            dve.wait_ge(S["rbr_in"], 16)
            past = lg[:, 0:UNITS, :]
            step(dve.tensor_tensor(past, ge.unsqueeze(2).to_broadcast([P, UNITS, H]),
                                   rbr[:, 0, :].unsqueeze(1).to_broadcast([P, UNITS, H]), ALU.add))
            step(dve.tensor_scalar(newsel[:], newsel[:], -1.0, -OFF, ALU.add, ALU.mult))
            step(dve.tensor_scalar(lg[:, UNITS, :], rbr[:, 0, :], const("nd")[:, 0:1], newsel[:, 0:1], ALU.mult, ALU.add))
            for b in range(1, DT):
                step(dve.scalar_tensor_tensor(out=lg[:, UNITS, :], in0=rbr[:, b, :], scalar=const("nd")[:, b:b + 1],
                                              in1=lg[:, UNITS, :], op0=ALU.mult, op1=ALU.add))
            step(dve.tensor_tensor(rbd[:, 1:NB, :], rbr[:, 1:NB, :], rbr[:, 0:NB - 1, :], ALU.subtract))
            for b in range(1, NB):
                step(dve.tensor_scalar(ge, dist[:], float(BUCKET_LO[b]), None, ALU.is_ge))
                step(dve.tensor_tensor(btmp, ge.unsqueeze(2).to_broadcast([P, UNITS, H]),
                                       rbd[:, b, :].unsqueeze(1).to_broadcast([P, UNITS, H]), ALU.mult))
                step(dve.tensor_tensor(past, past, btmp, ALU.add))

            dve.wait_ge(S["bias_in"], 16)
            dve.wait_ge(S["nat_copied"], 21)
            with dve.Fori(0, H // 2) as t:
                step.enter(t, 12)
                for e in range(2):
                    lp = lps[e]
                    dve.wait_ge(S["plog_done"], t * 2 + (e + 1))
                    step(dve.scalar_tensor_tensor(out=lp[:, 0:P], in0=bank(4, 0, P), scalar=QKS,
                                                  in1=biasW[:, bass.ds(t * 2 + e, 1), P:SEQ].rearrange("p a b -> p (a b)"),
                                                  op0=ALU.mult, op1=ALU.add))
                    dve.scalar_tensor_tensor(out=lp[:, P:3 * P], in0=bank(4, P, SEQ), scalar=QKS,
                                             in1=biasW[:, bass.ds(t * 2 + e, 1), :].rearrange("p a b -> p (a b)"),
                                             op0=ALU.mult, op1=ALU.add).then_inc(S["plog_read"], 1)
                    dve.wait_ge(S["plog_read"], t * 2 + (e + 1))
                    step(dve.tensor_tensor(lp[:], lp[:], mask2[:], ALU.add))
                    dve.tensor_reduce(qstep[:, 0:1], lp[:, 0:P], AX_X, ALU.max, negate=True)
                    dve.tensor_reduce(qstep[:, 1:2], lp[:, P:3 * P], AX_X, ALU.max, negate=True).then_inc(S["pmax_ready"], 1)
                    for g in range(2):
                        for r in range(4):
                            dve.wait_ge(ks[r], t * 64 + 16 * (2 * e + g + 1))
                            for h in range(H):
                                k_ = kv[:, r, h * HD:h * HD + HD]
                                m = dve.tensor_tensor_reduce(k_, k_, qrep[:, h * HD:h * HD + HD], 1.0, 0.0, ALU.mult, ALU.add,
                                                             lgt[:, r, h:h + 1])
                            m.then_inc(S["unit_read"], 1)
                        dve.wait_ge(S["unit_read"], t * 16 + (8 * e + 4 * g + 4))
                        at = bass.ds(t * 16 + (8 * e + 4 * g), 4)
                        step(dve.scalar_tensor_tensor(out=lg[:, at, :].rearrange("p a b -> p (a b)"), in0=lgt[:].rearrange("p a b -> p (a b)"),
                                                      scalar=QKS, in1=lg[:, at, :].rearrange("p a b -> p (a b)"), op0=ALU.mult, op1=ALU.add))
                    dve.wait_ge(S["pexp_done"], t * 4 + (2 * e + 2))
                    step(dve.reciprocal(qstep[:, 4:6], qstep[:, 2:4]))
                    step(dve.tensor_scalar(lp[:, 0:P], lp[:, 0:P], qstep[:, 4:5], None, ALU.mult))
                    dve.tensor_scalar(lp[:, P:3 * P], lp[:, P:3 * P], qstep[:, 5:6], None, ALU.mult).then_inc(S["pprob_ready"], 1)
                step.leave(H // 2)

            kcol = lgt[:, 0, :]
            for h in range(H):
                k_ = knrep[:, h * HD:h * HD + HD]
                m = dve.tensor_tensor_reduce(k_, k_, qrep[:, h * HD:h * HD + HD], 1.0, 0.0, ALU.mult, ALU.add, lgt[:, 0, h:h + 1])
            step(m)
            step(dve.scalar_tensor_tensor(out=lg[:, UNITS, :], in0=kcol, scalar=QKS, in1=lg[:, UNITS, :], op0=ALU.mult, op1=ALU.add))
            byh = lg[:].rearrange("p u h -> p h u")
            dve.tensor_reduce(small[:, 0:H], byh, AX_X, ALU.max).then_inc(S["tmax_ready"], 1)

            dve.wait_ge(S["win_evac"], 28)
            dve.wait_ge(S["pads_zero"], 1)
            cx = zB[:, CT:KT, :]
            step(dve.tensor_tensor(up[:, :, 2:SEQ + 2], cx[:, :, 0:SEQ], ccT[:, :, 0:SEQ], ALU.mult))
            for i in range(CT):
                m = dve.tensor_tensor(us[:, i, :, 2:6], cx[:, i, SEQ:TOK].rearrange("p (b t) -> p b t", b=DB),
                                      ccT[:, i, SEQ:TOK].rearrange("p (b t) -> p b t", b=DB), ALU.mult)
            step(m)
            dve.tensor_copy(ulast[:, :, 0:2], up[:, :, SEQ:SEQ + 2])
            dve.tensor_copy(ulast[:, :, 2:18].rearrange("p i (b j) -> p i b j", j=2), us[:, :, :, 4:6]).then_inc(S["ul_ready"], 1)
            for i in range(CT):
                for j in range(3):
                    tap = gcol[:, 3 * KT + CT * j + i:3 * KT + CT * j + i + 1]
                    pp, ps_ = cx[:, i, 0:SEQ], cx[:, i, SEQ:TOK].rearrange("p (b t) -> p b t", b=DB)
                    if j == 0:
                        dve.tensor_scalar(pp, up[:, i, 0:SEQ], tap, None, ALU.mult)
                        step(dve.tensor_scalar(ps_, us[:, i, :, 0:DT], tap, None, ALU.mult))
                    else:
                        dve.scalar_tensor_tensor(out=pp, in0=up[:, i, j:j + SEQ], scalar=tap, in1=pp, op0=ALU.mult, op1=ALU.add)
                        step(dve.scalar_tensor_tensor(out=ps_, in0=us[:, i, :, j:j + DT], scalar=tap, in1=ps_, op0=ALU.mult, op1=ALU.add))
            dve.tensor_tensor(cx, cx, cbT, ALU.mult).then_inc(S["conv_done"], 1)

            dve.wait_ge(S["tmax_turned"], 1)
            step(dve.tensor_reduce(smt, bank(4, 0, P, H).rearrange("p (n s) -> p n s", s=4), AX_X, ALU.max))
            dve.tensor_copy(smx.rearrange("p (n s) -> p n s", s=4), smt.unsqueeze(2).to_broadcast([H, NS, 4])).then_inc(S["tmax_wide"], 1)
            dve.wait_ge(S["tmax_back"], 1)
            dve.tensor_tensor(lg[:], lg[:], bank(7, 0, H).unsqueeze(1).to_broadcast([P, UNITS + 1, H]), ALU.subtract).then_inc(S["lg_shifted"], 1)
            dve.wait_ge(S["lg_exp"], 1)
            dve.tensor_reduce(small[:, 16:16 + H], byh, AX_X, ALU.add).then_inc(S["lsum_ready"], 1)
            dve.wait_ge(S["lsum_wide"], 1)
            step(dve.reciprocal(small[:, 32:32 + H], bank(4, 0, H)))
            step(dve.tensor_tensor(lg[:], lg[:], small[:, 32:32 + H].unsqueeze(1).to_broadcast([P, UNITS + 1, H]), ALU.mult))

            def spread(ring, col):
                dve.tensor_tensor(sp[:, ring], const("s32").unsqueeze(1).to_broadcast([P, H, NS]), col, ALU.mult).then_inc(S["sp_ready"], 1)

            dve.wait_ge(S["ul_turned"], 2)
            spread(0, lg[:, UNITS, :].unsqueeze(2).to_broadcast([P, H, NS]))

            dve.wait_ge(S["xh_ready"], 1)
            dve.tensor_tensor(XL[:, 0:CT, :], zB[:, CT:KT, :], XH[:, 0:CT, :], ALU.subtract).then_inc(S["xl_ready"], 1)

            def spread_turn(t, first):
                for r in range(4):
                    if not (first and r == 0):
                        dve.wait_ge(S["unit_summed"], t * 4 + r)
                    spread((1 + r) % 2, lg[:, bass.ds(t * 4 + r, 1), :].rearrange("p a h -> p (a h)").unsqueeze(2).to_broadcast([P, H, NS]))

            spread_turn(0, True)
            with dve.Fori(1, UNITS // 4) as t:
                spread_turn(t, False)

            def low(i, n):
                dve.wait_ge(S["wh_ready"], n)
                dve.tensor_tensor(WL[:, i % 2], wring[:, i % 2], WH[:, i % 2], ALU.subtract).then_inc(S["wl_ready"], 1)

            dve.wait_ge(S["ot_done"], 1)
            dve.wait_ge(S["u_out"], 32)
            low(0, 1)
            low(1, 2)
            dve.wait_ge(S["xh_ready"], 2)
            dve.tensor_tensor(XL[:, CT:KT, :], zB[:, 0:H, :], XH[:, CT:KT, :], ALU.subtract).then_inc(S["xl_ready"], 1)

            dve.wait_ge(S["win_evac"], NPAIR)
            with dve.Fori(0, 4) as t:
                step.enter(t, 4)
                for n in range(2):
                    for i in range(2):
                        low(i, t * 4 + (2 * n + i + 3))
                    dve.wait_ge(S["chunk_used"], t * 4 + (C_MIX + 2 * n + 2))
                    ga, gb = (g[:, bass.ds(t * 4 + 2 * n, 2), :] for g in (GA, GB))
                    step(dve.tensor_tensor(gb, gb, PM[:, 4 * n:4 * n + 2, 0:TOK], ALU.mult))
                    step(dve.tensor_tensor(ga, ga, PM[:, 4 * n + 2:4 * n + 4, 0:TOK], ALU.mult))
                    dve.tensor_tensor(ga, ga, gb, ALU.add).then_inc(S["mix_sum"], 1)
                    dve.wait_ge(S["yh_ready"], t * 2 + (n + 1))
                    yh, yl = (g[:, bass.ds(t * 4 + 2 * n, 2), :] for g in (YH, YL))
                    dve.tensor_tensor(yl, ga, yh, ALU.subtract).then_inc(S["yl_ready"], 1)
                step.leave(4)

            def residual(base, last=False):
                def pair(t, i, ahead=True):
                    if ahead:
                        for j in range(2):
                            low(j, t * 4 + (base - C_MIX + 2 * i + j + 3))
                    dve.wait_ge(S["chunk_used"], t * 4 + (base + 2 * i + 2))
                    x2 = xT[:, bass.ds(t * 4 + 2 * i, 2), :]
                    dve.tensor_tensor(x2, x2, PM[:, 2 * i:2 * i + 2, 0:TOK], ALU.add).then_inc(S["res_add"], 1)

                with dve.Fori(0, 3 if last else 4) as t:
                    for i in range(2):
                        pair(t, i)
                if last:
                    pair(3, 0)
                    pair(3, 1, False)

            residual(C_WO)
            dve.wait_ge(S["res_add"], 8)
            normalise(1)
            for k in range(0, KT, 2):
                dve.wait_ge(S["xh_ready"], 2 + k // 2 + 1)
                dve.tensor_tensor(XL[:, k:k + 2, :], hN[:, k:k + 2, :], XH[:, k:k + 2, :], ALU.subtract).then_inc(S["xl_ready"], 1)
            for f in range(DFF // D):
                base = C_MLP + 32 * f
                with dve.Fori(0, 4) as t:
                    step.enter(t, 2)
                    for i in range(2):
                        for j in range(2):
                            low(j, t * 4 + (base - C_MIX + 2 * i + j + 3))
                        dve.wait_ge(S["yh_ready"], t * 2 + (8 * (f + 1) + i + 1))
                        step(dve.tensor_tensor(tr[:, i], tr[:, i], tr[:, i], ALU.mult))
                        yh, yl = (g[:, bass.ds(t * 4 + 2 * i, 2), :] for g in (YH, YL))
                        dve.tensor_tensor(yl, tr[:, i], yh, ALU.subtract).then_inc(S["yl_ready"], 1)
                    step.leave(4)
                dve.wait_ge(S["res_add"], 8 * (f + 1))
                residual(base + 16, f == DFF // D - 1)
            dve.wait_ge(S["res_add"], 40)
            normalise(2)
            for n in range(12):
                rows = P if n < 8 else NS
                dst = ynat[:, n // 4, 512 * (n % 4):512 * (n % 4) + 512] if n < 8 else ysam[:, 512 * (n % 4):512 * (n % 4) + 512]
                dve.wait_ge(S["y_turned"], n + 1)
                dve.tensor_copy(dst, bank(n % 4, rows=rows)).then_inc(S["y_copied"], 1)

        @block.gpsimd
        def _(pool):
            pool.wait_ge(S["prow_ready"], 1)
            for b in range(DB):
                pool.indirect_dma_start(out=rawk[b].rearrange("p a b -> p (a b)"), out_offset=None, in_=I["cache_kidx"],
                                        in_offset=bass.IndirectOffsetOnAxis(ap=prow[:, b:b + 1], axis=0)).then_inc(pages_in[b], 16)
            pool.wait_ge(S["nat_done"], 14)
            pool.memset(up[:, :, 0:2], 0.0).then_inc(S["pads_zero"], 1)
            pool.wait_ge(S["spread_read"], 1)
            pool.wait_ge(S["nat_copied"], 21)
            pool.wait_ge(S["kv_out"], 32)

            for n in range(2 * UNITS):
                src, u = ("cache_k", n) if n < UNITS else ("cache_v", n - UNITS)
                if 4 <= n < UNITS + 4:
                    pool.wait_ge(S["unit_read"], n - 3)
                elif n >= UNITS + 4:
                    pool.wait_ge(S["unit_summed"], u - 2)
                pool.indirect_dma_start(out=kv[:, n % 4, :], out_offset=None, in_=I[src],
                                        in_offset=bass.IndirectOffsetOnAxis(ap=offs[:, u:u + 1], axis=0)).then_inc(ks[n % 4], 16)


def constants():
    import numpy as np
    f = np.float32
    p, n32 = np.arange(P), np.arange(NS)
    c = {}
    c["ident"] = np.eye(P)
    rs = np.zeros((P, 4, P))
    for s in range(4):
        rs[:NS, s] = (p[None, :] == 4 * n32[:, None] + s)
    c["rs"] = rs.reshape(P, -1)
    c["rall"] = rs.sum(1)
    rnew = np.zeros((P, P))
    rnew[:NS] = (n32[:, None] // 4 == p[None, :] // 16) & (n32[:, None] % 4 == p[None, :] % 4)
    c["rnew"] = rnew
    c["s32"] = (p[:, None] // 4 == n32[None, :])
    c["b4"] = (p[:, None] // 4 == p[None, :] // 4)
    ok = np.zeros((P, 4))
    ok[:NS] = np.arange(4)[None, :] <= (n32 % 4)[:, None]
    c["ok4"] = ok
    c["iota"] = np.broadcast_to(np.arange(NPG), (P, NPG))
    c["tpos"] = (PAST + (p // 4) % 4)[:, None]
    c["nd"] = (np.maximum((p // 4) % 4 - p % 4, 0)[:, None] == np.arange(DT)[None, :])
    far = np.maximum(SEQ - 1 - np.arange(TW), 0)
    lo = np.array(BUCKET_LO)
    bucket = (far[None, :] >= lo[:, None]).sum(0) - 1
    oh = np.zeros((P, TW))
    oh[:NB] = bucket[None, :] == np.arange(NB)[:, None]
    c["onehot"] = oh
    am = np.zeros((P, DB, 2, IH, DT))
    for e in range(2):
        for b in range(DB):
            for t in range(DT):
                am[NS * e + DT * b + t, b, e, :, t] = 1
    c["amask"] = am.reshape(P, -1)
    pg = np.zeros((P, P))
    pg[:NPG] = np.arange(NPG)[:, None] == p[None, :] // 8
    c["pgsel"] = pg
    c["r8"] = (p % 8)[:, None]
    k = np.arange(SEQ)
    c["causal"] = np.concatenate([p[:, None] >= p[None, :], P + p[:, None] >= k[None, :]], 1)
    pack = lambda lay: np.ascontiguousarray(np.concatenate([np.asarray(c[n], f) for n, _ in lay], 1))
    return pack(CONST_P), pack(CONST_E)


_SHAPES = {"x_prompt": (SEQ, D), "x_sample": (NS, D), "cache_k": (POOL * PS, AW), "cache_v": (POOL * PS, AW),
           "cache_kidx": (POOL * 8, PS // 8 * ID), "state_conv": (DB * 2, CW), "page_table": (DB, NPG), "rel_bias": (NB, H),
           "norm_mix_g": (1, D), "w_in": (D, NIN), "conv_w": (3, CW), "w_pa": (AW, D), "w_pb": (CW, D), "w_o": (D, D),
           "norm_mlp_g": (1, D), "w_mlp_in": (D, DFF), "w_mlp_out": (DFF, D), "norm_final_g": (1, D)}
_OUTS = [("y_prompt", (SEQ, D), (1, SEQ, D)), ("y_sample", (NS, D), (DB, DT, D)),
         ("k_prompt", (SEQ, AW), (1, 1, SEQ, H, HD)), ("v_prompt", (SEQ, AW), (1, 1, SEQ, H, HD)),
         ("kidx_prompt", (SEQ, ID), (1, 1, SEQ, ID)), ("conv_prompt", (2, CW), (1, 1, 2, CW)),
         ("k_sample", (NS, AW), (1, DB, DT, H, HD)), ("v_sample", (NS, AW), (1, DB, DT, H, HD)),
         ("kidx_sample", (NS, ID), (1, DB, DT, ID)), ("conv_sample", (DB * 2, CW), (1, DB, 2, CW))]


def kernel(**inputs):
    import numpy as np
    import concourse.bacc as bacc
    from concourse.bass_utils import run_bass_kernel_spmd as run

    nc = bacc.Bacc("TRN2", target_bir_lowering=False, num_devices=1)
    arrays, I = {}, {}
    for name, shape in _SHAPES.items():
        arrays[name] = np.ascontiguousarray(inputs[name]).reshape(shape)
    arrays["const_p"], arrays["const_e"] = constants()
    for name, a in arrays.items():
        I[name] = nc.dram_tensor(name, a.shape, mybir.dt.from_np(a.dtype), kind="ExternalInput").ap()
    O = {name: nc.dram_tensor("out_" + name, shape, F32, kind="ExternalOutput").ap() for name, shape, _ in _OUTS}
    build(nc, I, O)
    r = run(nc, [arrays], core_ids=[0])
    return tuple(r.results[0]["out_" + name].reshape(shape) for name, _, shape in _OUTS)
```

```python
from contextlib import ExitStack

import concourse.bass as bass
from concourse import mybir

ALU = mybir.AluOpType
ACT = mybir.ActivationFunctionType
F32 = mybir.dt.float32
I32 = mybir.dt.int32
F32R = mybir.dt.float32r
U32 = mybir.dt.uint32
AX_X = mybir.AxisListType.X

P = 128
D = 2048
KT = D // P
SEQ = 256
DB, DT = 8, 4
NS = DB * DT
TOK = SEQ + NS
H, HD = 8, 128
AW = H * HD
IH, ID = 16, 64
CW = 1024
CT = CW // P
DFF = 4 * D
PAST, PS = 2048, 128
NPG = PAST // PS
POOL = DB * NPG * 5 // 4
TOPK = 256
TOPP = 64
NB = 32
UNITS = TOPK // 4
NEG = -3.0e38
MARK = -3.3e38
CUT = -3.2e38
OFF = -1.0e30
EPS = 1e-6
QKS = float(HD) ** -0.5
BUCKET_LO = list(range(17)) + [19, 21, 24, 27, 31, 35, 40, 46, 52, 59, 67, 77, 87, 99, 113]

CK = 8
CN = 256
RING = 4
TW = 384

Q0, K0, V0, QI0, KI0 = 0, AW, 2 * AW, 3 * AW, 4 * AW
WI0 = KI0 + ID
CX0 = WI0 + IH
CB0, CC0, GA0 = CX0 + CW, CX0 + 2 * CW, CX0 + 3 * CW
GB0 = GA0 + D
NIN = GB0 + D
SEGS = [QI0, Q0, K0, V0, CX0, CC0, CB0]

CONST_P = [("ident", P), ("rs", 4 * P), ("rall", P), ("rnew", P), ("s32", NS), ("b4", P), ("ok4", 4),
           ("iota", NPG), ("tpos", 1), ("nd", DT)]
CONST_E = [("onehot", TW), ("amask", DB * P), ("causal", 3 * P), ("pgsel", P), ("r8", 1)]


def offsets(layout):
    at, out = 0, {}
    for name, n in layout:
        out[name] = (at, n)
        at += n
    return out, at


CP, CPW = offsets(CONST_P)
CE, CEW = offsets(CONST_E)


class Chain:

    def __init__(self, eng, sem):
        self.eng, self.sem, self.n, self.base = eng, sem, 0, None

    def __call__(self, ins):
        ins.then_inc(self.sem, 1)
        self.n += 1
        self.eng.wait_ge(self.sem, self.n if self.base is None else self.base + self.n)

    def enter(self, t, per):
        self.base, self.per, self.n0 = t * per, per, self.n

    def leave(self, times):
        assert self.n - self.n0 == self.per, (self.n - self.n0, self.per)
        self.n = self.n0 + self.per * times
        self.base = None


def build(nc, I, O):
    with ExitStack() as ctx:
        place = {}
        top = [-(-nc.sbuf_base // 64) * 64]

        def sb(name, shape, dt=F32, at=None):
            n = 4
            for d in shape[1:]:
                n *= d
            if at is None:
                at, top[0] = top[0], top[0] + -(-n // 32) * 32
            place[name] = at
            return nc.alloc_sbuf_tensor_at(name, shape, dt, offset=at)

        def view(t, a, shape, parts=P):
            n = 1
            for s in shape:
                n *= s
            v = t[0:parts, a:a + n]
            if len(shape) == 1:
                return v
            names = "abcd"[:len(shape)]
            return v.rearrange(f"p ({' '.join(names)}) -> p {' '.join(names)}", **dict(zip(names, shape)))

        wring = sb("wring", [P, RING, CK, CN])
        xT = sb("xT", [P, KT, TOK])
        hA = sb("hA", [P, KT, TOK])
        zB = sb("zB", [P, KT, TOK])
        G = sb("G", [P, 2 * KT * TOK])
        qT = sb("qT", [P, H, TOK])
        kT = sb("kT", [P, H, TOK])
        uv = sb("uv", [P, CT * (SEQ + 2) + CT * DB * 6])
        kv = sb("kv", [P, 4, AW])
        qrep = sb("qrep", [P, AW])
        knrep = sb("knrep", [P, AW])
        vnrep = sb("vnrep", [P, AW])
        scw = sb("scw", [P, PAST + 4])
        lg = sb("lg", [P, UNITS + 1, H])
        lgt = sb("lgt", [P, 4, H])
        mask2 = sb("mask2", [P, 3 * P])

        cp = sb("cp", [P, CPW])
        m8 = sb("m8", [P, 8])
        m8p = sb("m8p", [P, 8])
        ix = sb("ix", [NS, TOPK], U32)
        comb = sb("comb", [NS, 2 * UNITS + 1, 4])
        offs = sb("offs", [P, UNITS], U32)
        dist = sb("dist", [P, UNITS])
        newsel = sb("newsel", [P, 1])
        small = sb("small", [P, 64])
        rinv = sb("rinv", [P, TOK])
        gcol = sb("gcol", [P, 3 * KT + 3 * CT])
        wiN = sb("wiN", [P, 3, IH])
        kiT = sb("kiT", [P, TOK])
        kiN = sb("kiN", [P, 3, ID])
        sp = sb("sp", [P, 2, H, NS])
        qs2 = sb("qs2", [P, DB, IH, DT])
        var = mask2[:, 0:TOK]
        later = sb("later", [P, P])
        qstep = sb("qstep", [P, 8])
        rb = sb("rb", [NB, H])
        rbr = sb("rbr", [P, NB, H])
        ptf = sb("ptf", [NS, NPG])
        pti = sb("pti", [NS, NPG], I32)
        ptT = sb("ptT", [NPG, DB], I32)
        ptTf = sb("ptTf", [NPG, DB])
        prow = sb("prow", [P, DB], U32)
        ones = sb("ones", [P, P])
        eps = sb("eps", [P, 1])

        XH, XL = sb("XH", [P, KT, TOK], F32R, at=place["qT"]), sb("XL", [P, KT, TOK], F32R, at=place["uv"])
        YH, YL = sb("YH", [P, KT, TOK], F32R, at=place["hA"]), sb("YL", [P, KT, TOK], F32R, at=place["G"] + 4 * KT * TOK)
        WH = sb("WH", [P, 2, CK, CN], F32R, at=place["wring"] + 2 * 4 * CK * CN)
        WL = sb("WL", [P, 2, CK, CN], F32R, at=place["uv"] + 4 * KT * TOK)
        raw = [wring[:, i // 2, CK // 2 * (i % 2):CK // 2 * (i % 2) + CK // 2, :] for i in range(4)]
        VH = sb("VH", [P, 4, 2, CN], F32R, at=place["wring"] + 2 * 4 * CK * CN)
        VL = sb("VL", [P, 4, 2, CN], F32R, at=place["wring"] + 3 * 4 * CK * CN)
        hH, hL = sb("hH", [P, KT, TOK], F32R, at=place["xT"]), sb("hL", [P, KT, TOK], F32R, at=place["hA"])
        assert place["uv"] + 4 * KT * TOK + 4 * 2 * CK * CN <= place["vnrep"] + 4 * AW

        def flat(t):
            return t[:].rearrange("p a b -> p (a b)")

        zf, kvf, qf, kf = flat(zB), flat(kv), flat(qT), flat(kT)
        sc = scw[0:NS, :]
        btmp = view(scw, 0, [UNITS, H])
        rbd = view(scw, 512, [NB, H])
        pT = scw[:, 768:768 + 3 * P]
        lps = [scw[:, a:a + 3 * P] for a in (1152, 1536)]
        xin, xs = view(G, 0, [2, D]), view(G, 2 * D, [D], NS)
        qiT, ccT = view(G, 0, [H, TOK]), view(G, 0, [CT, TOK])
        biasW = view(G, 2304, [H, SEQ])
        Vp = view(G, 4352, [2, AW])
        Kn, cbT = view(G, 6400, [2, AW]), view(G, 6400, [CT, TOK])
        GA, GB = view(G, 0, [KT, TOK]), view(G, KT * TOK, [KT, TOK])
        ynat, ysam = view(G, KT * TOK, [2, D]), view(zf, 0, [D], NS)
        rawk = ([view(kvf, 1024 * b, [8, P]) for b in range(4)] + [view(G, 6144 + 1024 * b, [8, P]) for b in range(3)]
                + [view(zf, 2048, [8, P])])
        kiP = view(zf, 0, [2, PAST // 2])
        Amat = view(zf, 3072, [DB, P], 2 * NS)
        Wc = view(zf, 4096, [DB, 2 * NS])
        wk = view(qf, 0, [KT, 2 * ID + IH])
        ce = kf[:, 0:CEW]
        gN = kf[0:3 * KT + 3 * CT, CEW:CEW + P]
        hN = GA
        tr = view(zf, 0, [2, 2, TOK])
        sq = zB
        stN = kvf[0:2 * DB, 3 * AW:4 * AW]
        table = view(uv, 0, [4, TW])
        rl = view(uv, 0, [2, 512])
        rlp = view(uv, 1024, [2, 3 * P])
        vT = view(uv, 0, [H, TOK])
        up = view(uv, 0, [CT, SEQ + 2])
        us = view(uv, CT * (SEQ + 2), [CT, DB, 6])
        qn, kn, vn = (kv[0:NS, i, :] for i in range(3))
        ulast = view(sp[:].rearrange("p a h n -> p (a h n)"), 0, [CT, 18])
        qswap = view(sp[:].rearrange("p a h n -> p (a h n)"), 0, [H, NS])
        uN = knrep[0:18, :]
        eq, eqp = sc[:, 0:1024].rearrange("p (u g) -> p u g", g=NPG), sc[:, 1024:2048].rearrange("p (u g) -> p u g", g=NPG)
        osb = qrep[0:NS, :]
        smx, smt = lps[0][0:H, 0:P], lps[0][0:H, P:P + NS]

        def const(name, rows=P):
            where, t = (CP, cp) if name in CP else (CE, ce)
            a, n = where[name]
            return t[0:rows, a:a + n]

        PM = ctx.enter_context(nc.psum_tensor("PM", [P, 8, 512], F32))

        S = {n: ctx.enter_context(nc.semaphore(n)) for n in (
            "x_in consts_in early_in wk_in rb_in rbr_in gains_in state_in pt_in qs_moved qs_copied "
            "x_turned x_copied gains_turned gains_copied sq_ready sumsq rms_ready h_ready "
            "kiwi_done kiwi_copied kin_turned kin_copied kin_out amat_ready wc_turned wc_copied "
            "tab_done tab_copied bias_in consts_set early_free "
            "win_evac chunk_used "
            "pscore_done pscore_relu pscore_acc kp_turned kp_copied sscore_done sscore_relu scomb_done scomb_added "
            "nat_done nat_copied k_out kv_out comb_ready spread_done spread_read pads_zero "
            "plog_done plog_read pmax_ready pexp_done pprob_ready pt_turned pt_copied po_done po_copied "
            "unit_read conv_done tmax_ready tmax_turned tmax_wide tmax_back lg_shifted lg_exp lsum_ready lsum_wide "
            "sp_ready unit_summed o_copied ot_done ot_copied "
            "ul_ready ul_turned ul_copied u_out res_add relu_raw y_turned y_copied y_out "
            "ptT_in ptT_ready prow_sum prow_ready wh_ready wl_ready xh_ready xl_ready yh_ready yl_ready mix_sum dve_step "
            "ident_in y_moved x_saved x_back hh_ready hl_ready vh_ready vl_ready").split()}
        ld = [ctx.enter_context(nc.semaphore(f"weights_in{i}")) for i in range(RING)]
        ks = [ctx.enter_context(nc.semaphore(f"rows_in{i}")) for i in range(4)]
        pages_in = [ctx.enter_context(nc.semaphore(f"pages_in{i}")) for i in range(DB)]
        tabs = [ctx.enter_context(nc.semaphore(f"table_out{i}")) for i in range(4)]
        x_store = nc.dram_tensor("x_store", [P, KT * TOK], F32, kind="Internal").ap()
        scratch = nc.dram_tensor("bias_scratch", [H, P * (TW + 1)], F32, kind="Internal").ap()

        NPAIR = 4 * len(SEGS) + 16
        UNIT = 8
        C_MIX = UNIT * NPAIR
        C_WO = C_MIX + 16
        C_MLP = C_WO + 16

        block = ctx.enter_context(nc.Block())

        @block.sync
        def _(eng):
            def load(out, name, pair, a, k, sem):
                src = I[name][bass.ds(pair, 1), :, a * CN:(a + k) * CN].rearrange("o p n -> p (o n)")
                eng.dma_start(out.rearrange("p k n -> p (k n)"), src).then_inc(sem, 16)

            def win(p, t=None):
                for i in range(4):
                    if t is not None:
                        eng.wait_ge(S["vl_ready"], t * UNIT + (UNIT * p + 2 * i - 6))
                    elif p:
                        eng.wait_ge(S["vl_ready"], UNIT * p + 2 * i - 6)
                    load(raw[i], "w_in", p if t is None else t + p, CK // 2 * i, CK // 2, ld[i])

            eng.dma_start(xin[:, 0, :], I["x_prompt"][0:P, :]).then_inc(S["x_in"], 16)
            eng.dma_start(wk, I["w_kiwi"].rearrange("p (k n) -> p k n", k=KT)).then_inc(S["wk_in"], 16)
            win(0)
            with eng.Fori(1, NPAIR) as t:
                win(0, t)
            def turn2(chunks, split):
                for i, (name, pair, a) in enumerate(chunks):
                    if split is None and i < 2:
                        eng.wait_ge(S["vl_ready"], C_MIX - 4 + 2 * i + 2)
                    elif split is None:
                        eng.wait_ge(S["wl_ready"], i - 1)
                    else:
                        eng.wait_ge(S["wl_ready"], split + i)
                    load(wring[:, i % 2], name, pair, a, CK, ld[i % 2])

            def mix_chunks(t):
                return [("w_pa" if i % 2 else "w_pb", t * 2 + i // 2, 0) for i in range(4)]

            turn2(mix_chunks(0), None)
            eng.wait_ge(S["chunk_used"], C_MIX)
            eng.dma_start(xT[:].rearrange("p k n -> p (k n)"), x_store).then_inc(S["x_back"], 16)
            with eng.Fori(1, 4) as t:
                turn2(mix_chunks(t), t * 4 - 1)
            with eng.Fori(0, 4) as t:
                turn2([("w_o", t * 2 + i // 2, CK * (i % 2)) for i in range(4)], t * 4 + (C_WO - C_MIX - 1))
            for f in range(DFF // D):
                with eng.Fori(0, 4) as t:
                    turn2([("w_mlp_in", t * 2 + (8 * f + i // 2), CK * (i % 2)) for i in range(4)],
                          t * 4 + (C_MLP - C_MIX + 32 * f - 1))
                with eng.Fori(0, 4) as t:
                    turn2([("w_mlp_out", t * 2 + (8 * f + i // 2), CK * (i % 2)) for i in range(4)],
                          t * 4 + (C_MLP - C_MIX + 32 * f + 16 - 1))
            for j in range(6):
                part, c = j // 2, slice(D // 2 * (j % 2), D // 2 * (j % 2) + D // 2)
                eng.wait_ge(S["y_copied"], j + 1)
                eng.wait_ge(S["y_moved"], j + 1)
                if part < 2:
                    eng.dma_start(O["y_prompt"][part * P:part * P + P, c], ynat[:, part, c]).then_inc(S["y_out"], 16)
                else:
                    eng.dma_start(O["y_sample"][:, c], ysam[:, c]).then_inc(S["y_out"], 16)
            eng.wait_ge(S["y_out"], 96)

        @block.tensor
        def _(pe):
            def bank(i, a=0, n=512, rows=P, r0=0):
                return PM[r0:r0 + rows, i, a:a + n]

            def transpose(out, in_):
                n = in_.shape[0]
                return pe.transpose(out, in_, cp[0:n, 0:n])

            def win_half(p, half, t=None):
                def at(scale, n):
                    return n if t is None else t * scale + n
                if half == 0 and (p >= 2 or t is not None):
                    pe.wait_ge(S["win_evac"], at(2, p - 1))
                for j in range(4):
                    pe.wait_ge(S["vl_ready"], at(2 * UNIT, UNIT * p + 4 * half + j + 1))
                    if p == 0 and t is None:
                        pe.wait_ge(S["hl_ready"], CK * half + 2 * j + 2)
                    for o in range(2):
                        out = bank(2 * (p % 2) + o, 0, TOK)
                        for n in range(2):
                            k = CK * half + 2 * j + n
                            vh, vl = (v[:, j, n, o * P:o * P + P] for v in (VH, VL))
                            pe.matmul(out, vh, hH[:, k, :], start=(k == 0), stop=False)
                            pe.matmul(out, vh, hL[:, k, :], start=False, stop=False)
                            m = pe.matmul(out, vl, hH[:, k, :], start=False, stop=(k == KT - 1))
                    m.then_inc(S["chunk_used"], 1)

            def win_turns(p0, times, between=None):
                with pe.Fori(0, times) as t:
                    for i in range(4):
                        win_half(p0 + i // 2, i % 2, t)
                        if between:
                            between(t, i)

            def product3(i, split, b0, rhs, k0, first, last):
                pe.wait_ge(S["wl_ready"], split)
                rh, rl_ = rhs
                for o in range(2):
                    for k in range(CK):
                        wh, wl = (w[:, i % 2, k, o * P:o * P + P] for w in (WH, WL))
                        out = bank(b0 + o, 0, TOK)
                        pe.matmul(out, wh, rh[:, k0 + k, :], start=(first and k == 0), stop=False)
                        pe.matmul(out, wh, rl_[:, k0 + k, :], start=False, stop=False)
                        m = pe.matmul(out, wl, rh[:, k0 + k, :], start=False, stop=(last and k == CK - 1))
                m.then_inc(S["chunk_used"], 1)

            def wide(base, rhs, done, n0, before, m0, norm=None):
                def turn(t, first):
                    for i in range(4):
                        if first:
                            pe.wait_ge(before, m0 - 1 if i == 0 else m0)
                            if norm is not None and i < 2:
                                pe.wait_ge(S["xl_ready"], norm + 4 * (i + 1))
                        elif i % 2 == 0:
                            pe.wait_ge(done, t * 2 + (n0 + i // 2 - 1))
                        product3(i, t * 4 + (base - C_MIX + i + 1), 2 * (i // 2), rhs, CK * (i % 2), i % 2 == 0, i % 2 == 1)
                turn(0, True)
                with pe.Fori(1, 4) as t:
                    turn(t, False)

            def sum_squares(n, b):
                for k in range(KT):
                    pe.wait_ge(S["sq_ready"], KT * n + k + 1)
                    m = pe.matmul(bank(b, 0, TOK), ones[:], (sq if n else hA)[:, k, :], start=(k == 0), stop=(k == KT - 1))
                m.then_inc(S["sumsq"], 1)

            pe.wait_ge(S["ident_in"], 16)
            pe.wait_ge(S["x_in"], 48)
            for k in range(KT):
                if k >= 8:
                    pe.wait_ge(S["x_copied"], k - 7)
                for q in range(2):
                    transpose(bank(k % 8, q * P, P), xin[:, q, k * P:k * P + P])
                transpose(bank(k % 8, SEQ, NS), xs[:, k * P:k * P + P]).then_inc(S["x_turned"], 1)
            pe.wait_ge(S["x_copied"], KT)
            pe.wait_ge(S["gains_in"], 64)
            transpose(bank(0, 0, 3 * KT + 3 * CT), gN).then_inc(S["gains_turned"], 1)
            pe.wait_ge(S["consts_set"], 2)
            sum_squares(0, 1)

            pe.wait_ge(S["early_in"], 16)
            pe.wait_ge(S["ptT_ready"], 1)
            pe.matmul(bank(5, 0, DB), const("pgsel", NPG), ptTf[:], start=True, stop=True).then_inc(S["prow_sum"], 1)

            pe.wait_ge(S["rb_in"], 16)
            for h in range(H):
                if h >= 2:
                    pe.wait_ge(S["tab_copied"], h - 1)
                pe.matmul(bank(6 + h % 2, 0, TW), rb[:, h:h + 1].to_broadcast([NB, P]), const("onehot", NB),
                          start=True, stop=True).then_inc(S["tab_done"], 1)

            tok_tiles = ((0, P), (P, P), (SEQ, NS))
            pe.wait_ge(S["consts_in"], 16)
            pe.wait_ge(S["wk_in"], 16)
            for k in range(KT):
                pe.wait_ge(S["h_ready"], k + 1)
                pe.matmul(bank(2, 0, TOK), wk[:, k, 0:2 * ID], hA[:, k, :], start=(k == 0), stop=(k == KT - 1))
            for j, (a, n, r0) in enumerate(((0, P, 0), (P, P, 0), (SEQ, NS, 0), (SEQ, NS, NS))):
                for k in range(KT):
                    m = pe.matmul(bank(3, IH * min(j, 2), IH, n, r0), hA[:, k, a:a + n], wk[:, k, 2 * ID:2 * ID + IH],
                                  start=(k == 0), stop=(k == KT - 1))
            m.then_inc(S["kiwi_done"], 1)
            pe.wait_ge(S["kiwi_copied"], 3)
            for j, (a, n) in enumerate(tok_tiles):
                m = transpose(bank(4, ID * j, ID, n), kiT[0:ID, a:a + n])
            m.then_inc(S["kin_turned"], 1)
            pe.wait_ge(S["amat_ready"], 1)
            for j in range(DB):
                m = transpose(bank(5, 2 * NS * j, 2 * NS), Amat[:, j, :])
            m.then_inc(S["wc_turned"], 1)

            for p in range(4):
                win_half(p, 0)
                win_half(p, 1)

            pe.wait_ge(S["win_evac"], 4)
            pe.wait_ge(S["tab_copied"], H)
            pe.wait_ge(S["wc_copied"], 1)
            for h in range(IH):
                r, j = ID * (h % 2), h // 2
                if h >= 4:
                    pe.wait_ge(S["pscore_relu"], h - 3)
                pe.matmul(bank(4 + h % 4, 0, P), qiT[r:r + ID, j, 0:P], kiT[r:r + ID, 0:P], start=True, stop=True)
                pe.matmul(bank(4 + h % 4, P, SEQ), qiT[r:r + ID, j, P:SEQ], kiT[r:r + ID, 0:SEQ],
                          start=True, stop=True).then_inc(S["pscore_done"], 1)

            pe.wait_ge(S["qs_copied"], 4)
            pe.wait_ge(S["pscore_relu"], IH)

            def turn_keys(b):
                pe.wait_ge(pages_in[b], 16)
                for c in range(2):
                    at = 2 * b + c
                    if at >= 3:
                        pe.wait_ge(S["kp_copied"], at - 2)
                    for g in range(4):
                        m = transpose(bank(4 + at % 3, g * P, P), rawk[b][:, 4 * c + g, :])
                    m.then_inc(S["kp_turned"], 1)

            def scores(b, c):
                at = 3 * b + c
                if at >= 2:
                    pe.wait_ge(S["sscore_relu"], at - 1)
                if c < 2:
                    pe.wait_ge(S["kp_copied"], 2 * b + 2)
                for e in range(2 if c < 2 else 1):
                    r = ID * e
                    rhs = kiP[r:r + ID, b % 2, 512 * c:512 * c + 512] if c < 2 else kiT[0:ID, SEQ + DT * b:SEQ + DT * b + DT]
                    m = pe.matmul(PM[r:r + ID, at % 2, 0:rhs.shape[1]], qs2[r:r + ID, b].rearrange("p h t -> p (h t)"), rhs,
                                  start=True, stop=True)
                m.then_inc(S["sscore_done"], 1)

            def combine(b, c):
                at = 3 * b + c
                pe.wait_ge(S["sscore_relu"], at + 1)
                if c < 2:
                    m = pe.matmul(bank(2 + c, 0, 512, 2 * NS), Wc[:, b, :], rl[:, at % 2, :], start=(b == 0), stop=(b == DB - 1))
                else:
                    m = pe.matmul(bank(7, 0, DT, NS), Wc[0:ID, b, 0:NS], rl[0:ID, at % 2, 0:DT], start=(b == 0), stop=(b == DB - 1))
                m.then_inc(S["scomb_done"], 1)

            turn_keys(0)
            for b in range(DB):
                if b + 1 < DB:
                    turn_keys(b + 1)
                scores(b, 0)
                scores(b, 1)
                combine(b, 0)
                scores(b, 2)
                combine(b, 1)
                combine(b, 2)
            pe.wait_ge(S["scomb_added"], 5)

            win_turns(4, 6)

            pe.wait_ge(S["win_evac"], 16)
            nat = [0]

            def next_bank():
                if nat[0] >= 4:
                    pe.wait_ge(S["nat_copied"], nat[0] - 3)
                nat[0] += 1
                return 4 + (nat[0] - 1) % 4

            for src in (vT, kT):
                for q in range(2):
                    for quad in range(2):
                        b = next_bank()
                        for i in range(4):
                            m = transpose(bank(b, i * P, P), src[:, 4 * quad + i, q * P:q * P + P])
                        m.then_inc(S["nat_done"], 1)
            for src in (qT, kT, vT):
                for quad in range(2):
                    b = next_bank()
                    for i in range(4):
                        m = transpose(bank(b, i * P, P, NS), src[:, 4 * quad + i, SEQ:TOK])
                    m.then_inc(S["nat_done"], 1)
            for j, (src, pick) in enumerate(((qn, "rall"), (kn, "rnew"), (vn, "rnew"))):
                pe.wait_ge(S["nat_copied"], 10 + 2 * j)
                for half in range(2):
                    b = next_bank()
                    pe.matmul(bank(b), const(pick, NS), src[:, 512 * half:512 * half + 512],
                              start=True, stop=True).then_inc(S["nat_done"], 1)
            pe.wait_ge(S["state_in"], 16)
            b = next_bank()
            for i in range(CT):
                m = transpose(bank(b, 2 * DB * i, 2 * DB), stN[:, i * P:i * P + P])
            m.then_inc(S["nat_done"], 1)

            for p in range(16, 20):
                win_half(p, 0)
                win_half(p, 1)
            pe.wait_ge(S["comb_ready"], 1)
            pe.wait_ge(S["nat_copied"], 21)
            for s in range(4):
                m = pe.matmul(bank(7, 0, 2 * UNITS + 1), const("rs", NS)[:, s * P:s * P + P], comb[:, :, s],
                              start=(s == 0), stop=(s == 3))
            m.then_inc(S["spread_done"], 1)

            def prompt_logits(h):
                if h:
                    pe.wait_ge(S["plog_read"], h)
                pe.matmul(bank(4, 0, P), qT[:, h, 0:P], kT[:, h, 0:P], start=True, stop=True)
                pe.matmul(bank(4, P, SEQ), qT[:, h, P:SEQ], kT[:, h, 0:SEQ], start=True, stop=True).then_inc(S["plog_done"], 1)

            def prompt_turn(h):
                pe.wait_ge(S["pprob_ready"], h + 1)
                if h:
                    pe.wait_ge(S["pt_copied"], h)
                for i in range(3):
                    m = transpose(bank(5, i * P, P), lps[h % 2][:, i * P:i * P + P])
                m.then_inc(S["pt_turned"], 1)

            def prompt_out(h):
                pe.wait_ge(S["pt_copied"], h + 1)
                if h:
                    pe.wait_ge(S["po_copied"], h)
                pe.matmul(bank(6, 0, SEQ), Vp[:, 0, h * HD:h * HD + HD], pT[:, 0:SEQ], start=True, stop=False)
                pe.matmul(bank(6, P, P), Vp[:, 1, h * HD:h * HD + HD], pT[:, SEQ:3 * P], start=False, stop=True).then_inc(S["po_done"], 1)

            for j in range(H):
                prompt_logits(j)
                win_half(20 + j, 0)
                if j:
                    prompt_turn(j - 1)
                win_half(20 + j, 1)
                if j:
                    prompt_out(j - 1)
            prompt_turn(H - 1)
            prompt_out(H - 1)

            def pairs(first, end):
                for p in range(first, end):
                    win_half(p, 0)
                    win_half(p, 1)

            pairs(28, 32)
            pe.wait_ge(S["ul_ready"], 1)
            pe.wait_ge(S["po_copied"], H)
            for half in range(2):
                for i in range(4):
                    m = transpose(bank(5 + half, i * P, P, 18), ulast[:, 4 * half + i, :])
                m.then_inc(S["ul_turned"], 1)
            pairs(32, 34)
            pe.wait_ge(S["tmax_ready"], 1)
            transpose(bank(4, 0, P, H), small[:, 0:H]).then_inc(S["tmax_turned"], 1)
            pairs(34, 35)
            pe.wait_ge(S["tmax_wide"], 1)
            transpose(bank(7, 0, H), smx).then_inc(S["tmax_back"], 1)
            pairs(35, 36)
            pe.wait_ge(S["lsum_ready"], 1)
            pe.matmul(bank(4, 0, H), const("b4"), small[:, 16:16 + H], start=True, stop=True).then_inc(S["lsum_wide"], 1)
            pe.wait_ge(S["ul_copied"], 2)

            def unit_sum(ring, rows, first=False):
                for h in range(H):
                    m = pe.matmul(PM[0:NS, 6 + h // 4, (h % 4) * HD:(h % 4) * HD + HD], sp[:, ring, h, :], rows[:, h * HD:h * HD + HD],
                                  start=(first and h % 4 == 0), stop=False, skip_group_check=True)
                m.then_inc(S["unit_summed"], 1)

            def v_units(t, i):
                for r in range(4):
                    pe.wait_ge(S["sp_ready"], t * 16 + (4 * i + r + 2))
                    pe.wait_ge(ks[r], t * 64 + 16 * (UNITS // 4 + i + 1))
                    unit_sum((1 + r) % 2, kv[:, r, :])

            pe.wait_ge(S["sp_ready"], 1)
            unit_sum(0, vnrep[:], True)
            win_turns(36, 4, v_units)
            pe.wait_ge(S["o_copied"], 1)
            for i in range(H):
                m = transpose(bank(4, i * NS, NS), osb[:, i * P:i * P + P])
            m.then_inc(S["ot_done"], 1)
            pe.wait_ge(S["ot_copied"], 1)

            pe.wait_ge(S["win_evac"], NPAIR)

            def mix_turn(t, first):
                for i in range(4):
                    if first and i < 2:
                        pe.wait_ge(S["xl_ready"], i + 1)
                    elif not first and i % 2 == 0:
                        pe.wait_ge(S["yl_ready"], t * 2 + (i // 2 - 1))
                    product3(i, t * 4 + (i + 1), 4 * (i // 2) + 2 * (i % 2), (XH, XL), CT * (i % 2), True, True)

            mix_turn(0, True)
            with pe.Fori(1, 4) as t:
                mix_turn(t, False)

            wide(C_WO, (YH, YL), S["res_add"], 0, S["yl_ready"], 8)
            sum_squares(1, 4)
            for f in range(DFF // D):
                wide(C_MLP + 32 * f, (XH, XL), S["yl_ready"], 8 * (f + 1), S["res_add"], 8 * (f + 1),
                     None if f else 2)
                wide(C_MLP + 32 * f + 16, (YH, YL), S["res_add"], 8 * (f + 1), S["yl_ready"], 8 * (f + 2))
            sum_squares(2, 4)
            n = 0
            for a, rows in tok_tiles:
                for quad in range(4):
                    if a == 0:
                        pe.wait_ge(S["h_ready"], 2 * KT + 4 * quad + 4)
                    if n >= 4:
                        pe.wait_ge(S["y_moved" if n % 2 else "y_copied"], (n - 4) // 2 + 1)
                    for i in range(4):
                        m = transpose(bank(n % 4, i * P, P, rows), hN[:, 4 * quad + i, a:a + rows])
                    m.then_inc(S["y_turned"], 1)
                    n += 1

        @block.scalar
        def _(act):
            def bank(i, a=0, n=512, rows=P, r0=0):
                return PM[r0:r0 + rows, i, a:a + n]

            def copy(out, in_, **kw):
                return act.activation(out, in_, ACT.Copy, **kw)

            act.dma_start(cp[:, 0:P], I["const_p"][:, 0:P]).then_inc(S["ident_in"], 16)
            act.dma_start(xin[:, 1, :], I["x_prompt"][P:SEQ, :]).then_inc(S["x_in"], 16)
            act.dma_start(xs, I["x_sample"]).then_inc(S["x_in"], 16)
            with nc.allow_non_contiguous_dma(reason="128 page numbers, turned"):
                act.dma_start(ptT[:], I["page_table"].rearrange("b g -> g b")).then_inc(S["ptT_in"], 16)
            act.dma_start(ce, I["const_e"]).then_inc(S["early_in"], 16)
            act.dma_start(cp[:, P:], I["const_p"][:, P:]).then_inc(S["consts_in"], 16)
            for i, (name, n) in enumerate((("norm_mix_g", KT), ("norm_mlp_g", KT), ("norm_final_g", KT), ("conv_w", 3 * CT))):
                act.dma_start(gN[KT * i:KT * i + n, :], I[name].rearrange("a (i p) -> (a i) p", p=P)).then_inc(S["gains_in"], 16)
            act.dma_start(rb[:], I["rel_bias"]).then_inc(S["rb_in"], 16)
            act.dma_start(rbr[:].rearrange("p a b -> p (a b)"),
                          I["rel_bias"].rearrange("(o a) b -> o (a b)", o=1).to_broadcast([P, NB * H])).then_inc(S["rbr_in"], 16)
            for t in range(DT):
                act.dma_start(pti[t:NS:DT, :], I["page_table"]).then_inc(S["pt_in"], 16)

            def square_pair(w, first):
                act.wait_ge(S["res_add"], first + w + 1)
                for k in (2 * w, 2 * w + 1):
                    act.activation(sq[:, k, :], xT[:, k, :], ACT.Square).then_inc(S["sq_ready"], 1)

            def root(n, b):
                act.wait_ge(S["sumsq"], n + 1)
                if n:
                    act.wait_ge(S["h_ready"], KT * n)
                act.activation(rinv[:], bank(b, 0, TOK), ACT.Sqrt, bias=eps[:, 0:1], scale=1.0 / D).then_inc(S["rms_ready"], 1)

            for k in range(KT):
                act.wait_ge(S["x_copied"], k + 1)
                act.activation(hA[:, k, :], xT[:, k, :], ACT.Square).then_inc(S["sq_ready"], 1)
            act.wait_ge(S["gains_turned"], 1)
            copy(gcol[:], bank(0, 0, 3 * KT + 3 * CT)).then_inc(S["gains_copied"], 1)
            act.wait_ge(S["consts_set"], 2)
            act.dma_start(x_store, xT[:].rearrange("p k n -> p (k n)")).then_inc(S["x_saved"], 16)
            root(0, 1)

            split = [0]

            def highs(end):
                for u in range(split[0], min(end, C_MIX)):
                    act.wait_ge(ld[u // 2 % 4], 16 * (u // 8 + 1))
                    if u >= 4:
                        act.wait_ge(S["chunk_used"], u - 3)
                    copy(VH[:, u % 4], raw[u // 2 % 4][:, 2 * (u % 2):2 * (u % 2) + 2, :]).then_inc(S["vh_ready"], 1)
                split[0] = max(split[0], min(end, C_MIX))

            act.wait_ge(S["x_saved"], 16)
            for k in range(KT):
                act.wait_ge(S["h_ready"], k + 1)
                copy(hH[:, k, :], hA[:, k, :]).then_inc(S["hh_ready"], 1)
            highs(4)

            for h in range(H):
                act.wait_ge(S["tab_done"], h + 1)
                if h >= 4:
                    act.wait_ge(tabs[h % 4], 16)
                copy(table[:, h % 4, :], bank(6 + h % 2, 0, TW)).then_inc(S["tab_copied"], 1)
                act.wait_ge(S["tab_copied"], h + 1)
                act.dma_start(scratch[h].rearrange("(p w) -> p w", w=TW + 1)[:, 0:TW], table[:, h % 4, :]).then_inc(tabs[h % 4], 16)
            for i in range(4):
                act.wait_ge(tabs[i], 32)
            act.dma_start(biasW, scratch[:, 0:P * TW].rearrange("h (p w) -> p h w", w=TW)[:, :, P - 1:P - 1 + SEQ]).then_inc(S["bias_in"], 16)

            act.wait_ge(S["kiwi_done"], 1)
            copy(kiT[:], bank(2, 0, TOK)).then_inc(S["kiwi_copied"], 1)
            wis = float(ID) ** -0.5 * float(IH) ** -0.5
            copy(wiN[:, 0:2, :], bank(3, 0, 2 * IH), scale=wis).then_inc(S["kiwi_copied"], 1)
            copy(wiN[0:2 * NS, 2, :], bank(3, 2 * IH, IH, 2 * NS), scale=wis).then_inc(S["kiwi_copied"], 1)
            act.wait_ge(S["kin_turned"], 1)
            copy(kiN[:, 0:2, :], bank(4, 0, 2 * ID)).then_inc(S["kin_copied"], 1)
            copy(kiN[0:NS, 2, :], bank(4, 2 * ID, ID, NS)).then_inc(S["kin_copied"], 1)
            act.wait_ge(S["kin_copied"], 2)
            act.dma_start(O["kidx_prompt"].rearrange("(q p) d -> p q d", p=P), kiN[:, 0:2, :]).then_inc(S["kin_out"], 16)
            act.dma_start(O["kidx_sample"], kiN[0:NS, 2, :]).then_inc(S["kin_out"], 16)
            act.wait_ge(S["wc_turned"], 1)
            copy(Wc.rearrange("p a b -> p (a b)"), bank(5, 0, 2 * DB * NS)).then_inc(S["wc_copied"], 1)

            def evac(p, out, func=ACT.Copy):
                highs(UNIT * p + 12)
                act.wait_ge(S["chunk_used"], UNIT * p + UNIT)
                act.activation(out, PM[:, 2 * (p % 2):2 * (p % 2) + 2, 0:TOK], func).then_inc(S["win_evac"], 1)

            for p in range(4):
                evac(p, qiT[:, 2 * p:2 * p + 2, :])
            act.wait_ge(S["win_evac"], 4)
            act.dma_start(qswap[0:ID], qiT[ID:P, :, SEQ:TOK]).then_inc(S["qs_moved"], 16)
            act.dma_start(qswap[ID:P], qiT[0:ID, :, SEQ:TOK]).then_inc(S["qs_moved"], 16)
            by = qs2[:].rearrange("p b (j e) t -> p e j b t", e=2)
            own = qiT[:, :, SEQ:TOK].rearrange("p j (b t) -> p j b t", b=DB)
            swapped = qswap.rearrange("p j (b t) -> p j b t", b=DB)
            for half, e, src in ((0, 0, own), (1, 1, own), (0, 1, swapped), (1, 0, swapped)):
                if src is swapped:
                    act.wait_ge(S["qs_moved"], 32)
                for j in range(H):
                    m = copy(by[ID * half:ID * half + ID, e, j], src[ID * half:ID * half + ID, j])
                m.then_inc(S["qs_copied"], 1)

            for h in range(IH):
                act.wait_ge(S["pscore_done"], h + 1)
                if h >= 2:
                    act.wait_ge(S["pscore_acc"], h - 1)
                act.activation(rlp[:, h % 2, :], bank(4 + h % 4, 0, 3 * P), ACT.Relu).then_inc(S["pscore_relu"], 1)
            for at in range(3 * DB):
                n, rows = (512, P) if at % 3 < 2 else (DT, ID)
                act.wait_ge(S["sscore_done"], at + 1)
                if at >= 2:
                    act.wait_ge(S["scomb_done"], at - 1)
                act.activation(rl[0:rows, at % 2, 0:n], bank(at % 2, 0, n, rows), ACT.Relu).then_inc(S["sscore_relu"], 1)
            act.wait_ge(S["kp_turned"], 16)
            act.dma_start(stN, I["state_conv"]).then_inc(S["state_in"], 16)

            for p in range(4, 8):
                evac(p, qT[:, 2 * (p - 4):2 * (p - 4) + 2, :])
            act.wait_ge(S["early_free"], 1)
            for p in range(8, 12):
                evac(p, kT[:, 2 * (p - 8):2 * (p - 8) + 2, :])
            act.wait_ge(S["pscore_acc"], IH)
            for p in range(12, 16):
                evac(p, vT[:, 2 * (p - 12):2 * (p - 12) + 2, :])

            def nat(n, out, in_):
                act.wait_ge(S["nat_done"], n + 1)
                copy(out, in_).then_inc(S["nat_copied"], 1)

            n = 0
            for dst in (Vp, Kn):
                for q in range(2):
                    for quad in range(2):
                        nat(n, dst[:, q, 512 * quad:512 * quad + 512], bank(4 + n % 4))
                        n += 1
            for dst in (qn, kn, vn):
                for quad in range(2):
                    nat(n, dst[:, 512 * quad:512 * quad + 512], bank(4 + n % 4, rows=NS))
                    n += 1
            for dst in (qrep, knrep, vnrep):
                for half in range(2):
                    nat(n, dst[:, 512 * half:512 * half + 512], bank(4 + n % 4))
                    n += 1
            nat(n, us[:, :, :, 0:2], bank(4 + n % 4, 0, 2 * CT * DB).rearrange("p (i b j) -> p i b j", i=CT, b=DB))
            act.wait_ge(S["nat_copied"], n + 1)
            act.dma_start(O["k_prompt"].rearrange("(q p) d -> p q d", p=P), Kn).then_inc(S["k_out"], 16)
            act.dma_start(O["v_prompt"].rearrange("(q p) d -> p q d", p=P), Vp).then_inc(S["k_out"], 16)
            act.dma_start(O["k_sample"], kn).then_inc(S["kv_out"], 16)
            act.dma_start(O["v_sample"], vn).then_inc(S["kv_out"], 16)

            for p in range(16, 20):
                evac(p, zB[:, CT + 2 * (p - 16):CT + 2 * (p - 16) + 2, :])

            def prompt_turned(h):
                act.wait_ge(S["pt_turned"], h + 1)
                if h:
                    act.wait_ge(S["po_done"], h)
                copy(pT[:], bank(5, 0, 3 * P)).then_inc(S["pt_copied"], 1)

            def prompt_copied(h):
                act.wait_ge(S["po_done"], h + 1)
                copy(zB[:, h, 0:SEQ], bank(6, 0, SEQ)).then_inc(S["po_copied"], 1)

            for j in range(H):
                if j:
                    prompt_turned(j - 1)
                    highs(UNIT * (20 + j) + 7)
                act.wait_ge(S["pmax_ready"], j + 1)
                for i, (a, b) in enumerate(((0, P), (P, 3 * P))):
                    act.activation(lps[j % 2][:, a:b], lps[j % 2][:, a:b], ACT.Exp, bias=qstep[:, i:i + 1],
                                   accum_out=qstep[:, 2 + i:3 + i]).then_inc(S["pexp_done"], 1)
                if j == 4:
                    act.wait_ge(S["k_out"], 32)
                evac(20 + j, (ccT if j < 4 else cbT)[:, 2 * (j % 4):2 * (j % 4) + 2, :])
                if j:
                    prompt_copied(j - 1)
            prompt_turned(H - 1)
            prompt_copied(H - 1)

            def gate(p):
                g = GA if p < 36 else GB
                evac(p, g[:, 2 * (p % 36 % 28):2 * (p % 36 % 28) + 2, :], ACT.Sigmoid)

            highs(UNIT * 30 + 4)
            act.wait_ge(S["conv_done"], 1)
            for p in range(28, 32):
                gate(p)
            for half in range(2):
                act.wait_ge(S["ul_turned"], half + 1)
                copy(uN[:, 512 * half:512 * half + 512], bank(5 + half, rows=18)).then_inc(S["ul_copied"], 1)
            act.wait_ge(S["ul_copied"], 2)
            act.dma_start(O["conv_prompt"], uN[0:2, :]).then_inc(S["u_out"], 16)
            act.dma_start(O["conv_sample"], uN[2:18, :]).then_inc(S["u_out"], 16)
            for p in range(32, 35):
                gate(p)
            act.wait_ge(S["lg_shifted"], 1)
            act.activation(lg[:], lg[:], ACT.Exp).then_inc(S["lg_exp"], 1)
            gate(35)
            act.activation(XH[:, 0:CT, :], zB[:, CT:KT, :], ACT.Copy).then_inc(S["xh_ready"], 1)
            for p in range(36, 44):
                gate(p)

            def high(c):
                n = c - C_MIX
                act.wait_ge(ld[n % 2], 16 * (NPAIR + n // 2 + 1))
                act.wait_ge(S["chunk_used"], c - 1)
                copy(WH[:, n % 2], wring[:, n % 2]).then_inc(S["wh_ready"], 1)

            def high_pair(c):
                if c < C_MLP + 32 * (DFF // D):
                    high(c)
                    high(c + 1)

            act.wait_ge(S["chunk_used"], C_MIX)
            high_pair(C_MIX)
            act.wait_ge(S["unit_summed"], UNITS + 1)
            copy(osb.rearrange("p (a b) -> p a b", a=2), PM[0:NS, 6:8, :]).then_inc(S["o_copied"], 1)
            act.wait_ge(S["ot_done"], 1)
            copy(zB[:, 0:H, SEQ:TOK], bank(4, 0, H * NS).rearrange("p (h n) -> p h n", h=H)).then_inc(S["ot_copied"], 1)
            act.wait_ge(S["ot_copied"], 1)
            act.activation(XH[:, CT:KT, :], zB[:, 0:H, :], ACT.Copy).then_inc(S["xh_ready"], 1)
            for n in range(8):
                high_pair(C_MIX + 2 * n + 2)
                act.wait_ge(S["mix_sum"], n + 1)
                copy(YH[:, 2 * n:2 * n + 2, :], GA[:, 2 * n:2 * n + 2, :]).then_inc(S["yh_ready"], 1)
            for w in range(8):
                high_pair(C_WO + 2 * w + 2)
                if w:
                    square_pair(w - 1, 0)
            square_pair(7, 0)
            root(1, 4)
            for k in range(0, KT, 2):
                act.wait_ge(S["h_ready"], KT + k + 2)
                copy(XH[:, k:k + 2, :], hN[:, k:k + 2, :]).then_inc(S["xh_ready"], 1)
            for f in range(DFF // D):
                for w in range(8):
                    n = 8 * f + w
                    high_pair(C_MLP + 32 * f + 2 * w + 2)
                    act.wait_ge(S["chunk_used"], C_MLP + 32 * f + 2 * w + 2)
                    if n >= 2:
                        act.wait_ge(S["yl_ready"], 8 + n - 1)
                    act.activation(tr[:, w % 2], PM[:, 2 * (w % 2):2 * (w % 2) + 2, 0:TOK], ACT.Relu).then_inc(S["relu_raw"], 1)
                    act.wait_ge(S["relu_raw"], n + 1)
                    act.activation(YH[:, 2 * w:2 * w + 2, :], tr[:, w % 2], ACT.Square).then_inc(S["yh_ready"], 1)
                for w in range(8):
                    high_pair(C_MLP + 32 * f + 16 + 2 * w + 2)
                    if w and f == DFF // D - 1:
                        square_pair(w - 1, 32)
            square_pair(7, 32)
            root(2, 4)
            for n in range(1, 12, 2):
                rows = P if n < 8 else NS
                dst = ynat[:, n // 4, 512 * (n % 4):512 * (n % 4) + 512] if n < 8 else ysam[:, 512 * (n % 4):512 * (n % 4) + 512]
                act.wait_ge(S["y_turned"], n + 1)
                copy(dst, bank(n % 4, rows=rows)).then_inc(S["y_moved"], 1)
            act.wait_ge(S["kin_out"], 32)
            act.wait_ge(S["kv_out"], 32)

        @block.vector
        def _(dve):
            step = Chain(dve, S["dve_step"])

            def bank(i, a=0, n=512, rows=P, r0=0):
                return PM[r0:r0 + rows, i, a:a + n]

            dve.memset(ones[:], 1.0).then_inc(S["consts_set"], 1)
            dve.memset(eps[:], EPS).then_inc(S["consts_set"], 1)
            for k in range(KT):
                dve.wait_ge(S["x_turned"], k + 1)
                dve.tensor_copy(xT[:, k, :], bank(k % 8, 0, TOK)).then_inc(S["x_copied"], 1)

            def normalise(n):
                dve.wait_ge(S["rms_ready"], n + 1)
                step(dve.tensor_scalar(var, bank(1 if n == 0 else 4, 0, TOK), -0.5 / D, -0.5 * EPS, ALU.mult, ALU.add))
                step(dve.reciprocal(rinv[:], rinv[:]))
                step(dve.tensor_tensor(var, var, rinv[:], ALU.mult))
                step(dve.tensor_tensor(var, var, rinv[:], ALU.mult))
                step(dve.scalar_tensor_tensor(out=rinv[:], in0=var, scalar=1.5, in1=rinv[:], op0=ALU.add, op1=ALU.mult))
                if n == 0:
                    dve.wait_ge(S["gains_copied"], 1)
                for k in range(KT):
                    dve.scalar_tensor_tensor(out=(hN if n else hA)[:, k, :], in0=xT[:, k, :], scalar=gcol[:, KT * n + k:KT * n + k + 1],
                                             in1=rinv[:], op0=ALU.mult, op1=ALU.mult).then_inc(S["h_ready"], 1)
                    if n == 1 and k % 2 and k > 1:
                        norm_low(k - 3)
                if n == 1:
                    norm_low(KT - 2)

            def norm_low(k):
                dve.wait_ge(S["xh_ready"], 2 + k // 2 + 1)
                dve.tensor_tensor(XL[:, k:k + 2, :], hN[:, k:k + 2, :], XH[:, k:k + 2, :], ALU.subtract).then_inc(S["xl_ready"], 1)

            dve.wait_ge(S["ptT_in"], 16)
            dve.tensor_copy(ptTf[:], ptT[:]).then_inc(S["ptT_ready"], 1)
            dve.wait_ge(S["x_copied"], KT)
            normalise(0)
            dve.wait_ge(S["early_in"], 16)
            dve.wait_ge(S["prow_sum"], 1)
            dve.tensor_scalar(prow[:], bank(5, 0, DB), 8.0, const("r8")[:, 0:1], ALU.mult, ALU.add).then_inc(S["prow_ready"], 1)

            dve.wait_ge(S["h_ready"], KT)
            step(dve.memset(mask2[:], 0.0))

            dve.wait_ge(S["kiwi_done"], 1)
            for k in range(KT):
                dve.wait_ge(S["hh_ready"], k + 1)
                dve.tensor_tensor(hL[:, k, :], hA[:, k, :], hH[:, k, :], ALU.subtract).then_inc(S["hl_ready"], 1)

            dve.wait_ge(S["early_in"], 16)
            dve.wait_ge(S["kiwi_copied"], 3)
            for j in range(DB):
                m = dve.tensor_tensor(Amat[:, j, :].rearrange("p (b h t) -> p b h t", b=2, h=IH),
                                      const("amask", 2 * NS)[:, P * j:P * j + P].rearrange("p (b h t) -> p b h t", b=2, h=IH),
                                      wiN[0:2 * NS, 2, :].unsqueeze(1).unsqueeze(3).to_broadcast([2 * NS, 2, IH, DT]), ALU.mult)
            m.then_inc(S["amat_ready"], 1)
            dve.wait_ge(S["pt_in"], 16 * DT)
            dve.tensor_copy(ptf[:], pti[:])

            for h in range(IH):
                dve.wait_ge(S["pscore_relu"], h + 1)
                if h:
                    dve.wait_ge(S["pscore_acc"], h)
                for q, (a, b) in enumerate(((0, P), (P, 3 * P))):
                    m = dve.scalar_tensor_tensor(out=mask2[:, a:b], in0=rlp[:, h % 2, a:b], scalar=wiN[:, q, h:h + 1],
                                                 in1=mask2[:, a:b], op0=ALU.mult, op1=ALU.add)
                m.then_inc(S["pscore_acc"], 1)
            dve.wait_ge(S["pscore_acc"], IH)
            step(dve.tensor_scalar(lps[0][:], const("causal"), -1.0, -NEG, ALU.add, ALU.mult))
            step(dve.tensor_scalar(later[:], const("causal")[:, 0:P], -1.0, -OFF, ALU.add, ALU.mult))
            step(dve.tensor_tensor(mask2[:], mask2[:], const("causal"), ALU.mult))
            dve.tensor_tensor(mask2[:], mask2[:], lps[0][:], ALU.add).then_inc(S["early_free"], 1)

            for at in range(2 * DB):
                b, c = at // 2, at % 2
                dve.wait_ge(S["kp_turned"], at + 1)
                if b >= 2:
                    dve.wait_ge(S["sscore_done"], 3 * (b - 1))
                dve.tensor_copy(kiP[:, b % 2, :].rearrange("x (p j) -> x p j", j=8)[:, :, 4 * c:4 * c + 4],
                                bank(4 + at % 3).rearrange("x (j p) -> x p j", j=4)).then_inc(S["kp_copied"], 1)
            dve.wait_ge(S["scomb_done"], 3 * DB)
            for c in range(2):
                for e in range(2):
                    dve.tensor_copy(sc[:, 1024 * c:1024 * c + 1024].rearrange("n (m e) -> n m e", e=2)[:, :, e],
                                    PM[NS * e:NS * e + NS, 2 + c, :]).then_inc(S["scomb_added"], 1)
            dve.tensor_copy(sc[:, PAST:], bank(7, 0, DT, NS)).then_inc(S["scomb_added"], 1)
            dve.wait_ge(S["scomb_added"], 5)
            step(dve.tensor_tensor(sc[:, PAST:], sc[:, PAST:], const("ok4", NS), ALU.mult))
            step(dve.tensor_scalar(m8[0:NS, 0:4], const("ok4", NS), -1.0, -NEG, ALU.add, ALU.mult))
            step(dve.tensor_tensor(sc[:, PAST:], sc[:, PAST:], m8[0:NS, 0:4], ALU.add))

            for i in range(TOPK // 8):
                step(dve.max(m8[0:NS, :], sc[:]))
                step(dve.max_index(ix[:, 8 * i:8 * i + 8], m8[0:NS, :], sc[:]))
                step(dve.match_replace(sc[:], m8[0:NS, :], sc[:], MARK))
            step(dve.tensor_scalar(comb[:, 2 * UNITS, :], sc[:, PAST:], CUT, None, ALU.is_le))
            pos = comb[:, UNITS:2 * UNITS, :].rearrange("p u s -> p (u s)")
            rows = comb[:, 0:UNITS, :].rearrange("p u s -> p (u s)")
            step(dve.tensor_copy(pos, ix[:]))
            step(dve.tensor_scalar(ix[:], ix[:], float(PAST - 1), None, ALU.min))
            step(dve.tensor_copy(rows, ix[:]))
            step(dve.tensor_scalar(ix[:], ix[:], 7, None, ALU.logical_shift_right))
            for a in range(0, TOPK, 64):
                step(dve.tensor_tensor(eq, ix[:, a:a + 64].unsqueeze(2).to_broadcast([NS, 64, NPG]),
                                       const("iota", NS).unsqueeze(1).to_broadcast([NS, 64, NPG]), ALU.is_equal))
                step(dve.tensor_tensor(eqp, eq, ptf[:].unsqueeze(1).to_broadcast([NS, 64, NPG]), ALU.mult))
                step(dve.tensor_reduce(eq[:, 0:4, :].rearrange("p u g -> p (u g)"), eqp, AX_X, ALU.add))
                flat_eq = eq[:, 0:4, :].rearrange("p u g -> p (u g)")
                step(dve.tensor_tensor(flat_eq, flat_eq, ix[:, a:a + 64], ALU.subtract))
                m = dve.scalar_tensor_tensor(out=rows[:, a:a + 64], in0=flat_eq, scalar=float(PS), in1=rows[:, a:a + 64],
                                             op0=ALU.mult, op1=ALU.add)
                if a + 64 < TOPK:
                    step(m)
            m.then_inc(S["comb_ready"], 1)

            for a, b in ((0, P), (P, 3 * P)):
                for i in range(TOPP // 8):
                    step(dve.max(m8p[:], mask2[:, a:b]))
                    step(dve.match_replace(mask2[:, a:b], m8p[:], mask2[:, a:b], MARK))
            step(dve.tensor_scalar(mask2[:], mask2[:], CUT, OFF, ALU.is_gt, ALU.mult))
            for a in (0, 2 * P):
                step(dve.tensor_tensor(mask2[:, a:a + P], mask2[:, a:a + P], later[:], ALU.add))

            dve.wait_ge(S["spread_done"], 1)
            dve.tensor_copy(offs[:], bank(7, 0, UNITS))
            dve.tensor_scalar(dist[:], bank(7, UNITS, UNITS), -1.0, const("tpos")[:, 0:1], ALU.mult, ALU.add)
            dve.tensor_copy(newsel[:], bank(7, 2 * UNITS, 1))
            ge = small[:, 0:UNITS]
            dve.tensor_scalar(ge, bank(7, UNITS, UNITS), PAST - 0.5, OFF, ALU.is_gt, ALU.mult).then_inc(S["spread_read"], 1)
            dve.wait_ge(S["spread_read"], 1)
            dve.wait_ge(S["rbr_in"], 16)
            past = lg[:, 0:UNITS, :]
            step(dve.tensor_tensor(past, ge.unsqueeze(2).to_broadcast([P, UNITS, H]),
                                   rbr[:, 0, :].unsqueeze(1).to_broadcast([P, UNITS, H]), ALU.add))
            step(dve.tensor_scalar(newsel[:], newsel[:], -1.0, -OFF, ALU.add, ALU.mult))
            step(dve.tensor_scalar(lg[:, UNITS, :], rbr[:, 0, :], const("nd")[:, 0:1], newsel[:, 0:1], ALU.mult, ALU.add))
            for b in range(1, DT):
                step(dve.scalar_tensor_tensor(out=lg[:, UNITS, :], in0=rbr[:, b, :], scalar=const("nd")[:, b:b + 1],
                                              in1=lg[:, UNITS, :], op0=ALU.mult, op1=ALU.add))

            dve.wait_ge(S["bias_in"], 16)
            dve.wait_ge(S["nat_copied"], 21)
            with dve.Fori(0, H // 2) as t:
                step.enter(t, 12)
                for e in range(2):
                    lp = lps[e]
                    dve.wait_ge(S["plog_done"], t * 2 + (e + 1))
                    step(dve.scalar_tensor_tensor(out=lp[:, 0:P], in0=bank(4, 0, P), scalar=QKS,
                                                  in1=biasW[:, bass.ds(t * 2 + e, 1), P:SEQ].rearrange("p a b -> p (a b)"),
                                                  op0=ALU.mult, op1=ALU.add))
                    dve.scalar_tensor_tensor(out=lp[:, P:3 * P], in0=bank(4, P, SEQ), scalar=QKS,
                                             in1=biasW[:, bass.ds(t * 2 + e, 1), :].rearrange("p a b -> p (a b)"),
                                             op0=ALU.mult, op1=ALU.add).then_inc(S["plog_read"], 1)
                    dve.wait_ge(S["plog_read"], t * 2 + (e + 1))
                    step(dve.tensor_tensor(lp[:], lp[:], mask2[:], ALU.add))
                    dve.tensor_reduce(qstep[:, 0:1], lp[:, 0:P], AX_X, ALU.max, negate=True)
                    dve.tensor_reduce(qstep[:, 1:2], lp[:, P:3 * P], AX_X, ALU.max, negate=True).then_inc(S["pmax_ready"], 1)
                    for g in range(2):
                        for r in range(4):
                            dve.wait_ge(ks[r], t * 64 + 16 * (2 * e + g + 1))
                            for h in range(H):
                                k_ = kv[:, r, h * HD:h * HD + HD]
                                m = dve.tensor_tensor_reduce(k_, k_, qrep[:, h * HD:h * HD + HD], 1.0, 0.0, ALU.mult, ALU.add,
                                                             lgt[:, r, h:h + 1])
                            m.then_inc(S["unit_read"], 1)
                        dve.wait_ge(S["unit_read"], t * 16 + (8 * e + 4 * g + 4))
                        at = bass.ds(t * 16 + (8 * e + 4 * g), 4)
                        step(dve.scalar_tensor_tensor(out=lg[:, at, :].rearrange("p a b -> p (a b)"), in0=lgt[:].rearrange("p a b -> p (a b)"),
                                                      scalar=QKS, in1=lg[:, at, :].rearrange("p a b -> p (a b)"), op0=ALU.mult, op1=ALU.add))
                    dve.wait_ge(S["pexp_done"], t * 4 + (2 * e + 2))
                    step(dve.reciprocal(qstep[:, 4:6], qstep[:, 2:4]))
                    step(dve.tensor_scalar(lp[:, 0:P], lp[:, 0:P], qstep[:, 4:5], None, ALU.mult))
                    dve.tensor_scalar(lp[:, P:3 * P], lp[:, P:3 * P], qstep[:, 5:6], None, ALU.mult).then_inc(S["pprob_ready"], 1)
                step.leave(H // 2)

            kcol = lgt[:, 0, :]
            for h in range(H):
                k_ = knrep[:, h * HD:h * HD + HD]
                m = dve.tensor_tensor_reduce(k_, k_, qrep[:, h * HD:h * HD + HD], 1.0, 0.0, ALU.mult, ALU.add, lgt[:, 0, h:h + 1])
            step(m)
            step(dve.scalar_tensor_tensor(out=lg[:, UNITS, :], in0=kcol, scalar=QKS, in1=lg[:, UNITS, :], op0=ALU.mult, op1=ALU.add))
            def unit_low(u, t=None):
                dve.wait_ge(S["vh_ready"], u + 1 if t is None else t * 8 + (u + 1))
                r = raw[u // 2 % 4][:, 2 * (u % 2):2 * (u % 2) + 2, :]
                dve.tensor_tensor(VL[:, u % 4], r, VH[:, u % 4], ALU.subtract).then_inc(S["vl_ready"], 1)

            U0 = UNIT * 28
            dve.wait_ge(S["win_evac"], 28)
            dve.wait_ge(S["pads_zero"], 1)
            cx = zB[:, CT:KT, :]
            step(dve.tensor_tensor(up[:, :, 2:SEQ + 2], cx[:, :, 0:SEQ], ccT[:, :, 0:SEQ], ALU.mult))
            for i in range(CT):
                m = dve.tensor_tensor(us[:, i, :, 2:6], cx[:, i, SEQ:TOK].rearrange("p (b t) -> p b t", b=DB),
                                      ccT[:, i, SEQ:TOK].rearrange("p (b t) -> p b t", b=DB), ALU.mult)
            step(m)
            dve.tensor_copy(ulast[:, :, 0:2], up[:, :, SEQ:SEQ + 2])
            dve.tensor_copy(ulast[:, :, 2:18].rearrange("p i (b j) -> p i b j", j=2), us[:, :, :, 4:6]).then_inc(S["ul_ready"], 1)
            for i in range(CT):
                for j in range(3):
                    tap = gcol[:, 3 * KT + CT * j + i:3 * KT + CT * j + i + 1]
                    pp, ps_ = cx[:, i, 0:SEQ], cx[:, i, SEQ:TOK].rearrange("p (b t) -> p b t", b=DB)
                    if j == 0:
                        dve.tensor_scalar(pp, up[:, i, 0:SEQ], tap, None, ALU.mult)
                        step(dve.tensor_scalar(ps_, us[:, i, :, 0:DT], tap, None, ALU.mult))
                    else:
                        dve.scalar_tensor_tensor(out=pp, in0=up[:, i, j:j + SEQ], scalar=tap, in1=pp, op0=ALU.mult, op1=ALU.add)
                        step(dve.scalar_tensor_tensor(out=ps_, in0=us[:, i, :, j:j + DT], scalar=tap, in1=ps_, op0=ALU.mult, op1=ALU.add))
            dve.tensor_tensor(cx, cx, cbT, ALU.mult).then_inc(S["conv_done"], 1)

            step(dve.tensor_tensor(rbd[:, 1:NB, :], rbr[:, 1:NB, :], rbr[:, 0:NB - 1, :], ALU.subtract))
            for b in range(1, NB):
                step(dve.tensor_scalar(ge, dist[:], float(BUCKET_LO[b]), None, ALU.is_ge))
                step(dve.tensor_tensor(btmp, ge.unsqueeze(2).to_broadcast([P, UNITS, H]),
                                       rbd[:, b, :].unsqueeze(1).to_broadcast([P, UNITS, H]), ALU.mult))
                step(dve.tensor_tensor(past, past, btmp, ALU.add))
            byh = lg[:].rearrange("p u h -> p h u")
            dve.tensor_reduce(small[:, 0:H], byh, AX_X, ALU.max).then_inc(S["tmax_ready"], 1)

            dve.wait_ge(S["tmax_turned"], 1)
            step(dve.tensor_reduce(smt, bank(4, 0, P, H).rearrange("p (n s) -> p n s", s=4), AX_X, ALU.max))
            dve.tensor_copy(smx.rearrange("p (n s) -> p n s", s=4), smt.unsqueeze(2).to_broadcast([H, NS, 4])).then_inc(S["tmax_wide"], 1)
            dve.wait_ge(S["tmax_back"], 1)
            dve.tensor_tensor(lg[:], lg[:], bank(7, 0, H).unsqueeze(1).to_broadcast([P, UNITS + 1, H]), ALU.subtract).then_inc(S["lg_shifted"], 1)
            dve.wait_ge(S["lg_exp"], 1)
            dve.tensor_reduce(small[:, 16:16 + H], byh, AX_X, ALU.add).then_inc(S["lsum_ready"], 1)
            dve.wait_ge(S["lsum_wide"], 1)
            step(dve.reciprocal(small[:, 32:32 + H], bank(4, 0, H)))
            step(dve.tensor_tensor(lg[:], lg[:], small[:, 32:32 + H].unsqueeze(1).to_broadcast([P, UNITS + 1, H]), ALU.mult))

            def spread(ring, col):
                dve.tensor_tensor(sp[:, ring], const("s32").unsqueeze(1).to_broadcast([P, H, NS]), col, ALU.mult).then_inc(S["sp_ready"], 1)

            dve.wait_ge(S["ul_turned"], 2)
            spread(0, lg[:, UNITS, :].unsqueeze(2).to_broadcast([P, H, NS]))

            dve.wait_ge(S["xh_ready"], 1)
            dve.tensor_tensor(XL[:, 0:CT, :], zB[:, CT:KT, :], XH[:, 0:CT, :], ALU.subtract).then_inc(S["xl_ready"], 1)

            def spread_turn(n, t=None):
                for v in range(4 * n, 4 * n + 4):
                    at = v if t is None else t * 8 + v
                    if v < UNITS - 4:
                        unit_low(U0 + 68 + v, t)
                    if v or t is not None:
                        dve.wait_ge(S["unit_summed"], at)
                    spread((1 + v) % 2, lg[:, bass.ds(at, 1), :].rearrange("p a h -> p (a h)").unsqueeze(2).to_broadcast([P, H, NS]))

            dve.wait_ge(S["vl_ready"], U0 + 68)
            spread_turn(0)
            with dve.Fori(0, UNITS // 8 - 1) as t:
                spread_turn(1, t)
                spread_turn(2, t)
            spread_turn(UNITS // 4 - 1)

            def low(i, n):
                dve.wait_ge(S["wh_ready"], n)
                dve.tensor_tensor(WL[:, i % 2], wring[:, i % 2], WH[:, i % 2], ALU.subtract).then_inc(S["wl_ready"], 1)

            dve.wait_ge(S["ot_done"], 1)
            dve.wait_ge(S["u_out"], 32)
            low(0, 1)
            low(1, 2)
            dve.wait_ge(S["xh_ready"], 2)
            dve.tensor_tensor(XL[:, CT:KT, :], zB[:, 0:H, :], XH[:, CT:KT, :], ALU.subtract).then_inc(S["xl_ready"], 1)

            dve.wait_ge(S["win_evac"], NPAIR)
            with dve.Fori(0, 4) as t:
                step.enter(t, 4)
                for n in range(2):
                    for i in range(2):
                        low(i, t * 4 + (2 * n + i + 3))
                    dve.wait_ge(S["chunk_used"], t * 4 + (C_MIX + 2 * n + 2))
                    ga, gb = (g[:, bass.ds(t * 4 + 2 * n, 2), :] for g in (GA, GB))
                    step(dve.tensor_tensor(gb, gb, PM[:, 4 * n:4 * n + 2, 0:TOK], ALU.mult))
                    step(dve.tensor_tensor(ga, ga, PM[:, 4 * n + 2:4 * n + 4, 0:TOK], ALU.mult))
                    dve.tensor_tensor(ga, ga, gb, ALU.add).then_inc(S["mix_sum"], 1)
                    dve.wait_ge(S["yh_ready"], t * 2 + (n + 1))
                    yh, yl = (g[:, bass.ds(t * 4 + 2 * n, 2), :] for g in (YH, YL))
                    dve.tensor_tensor(yl, ga, yh, ALU.subtract).then_inc(S["yl_ready"], 1)
                step.leave(4)

            def residual(base, last=False):
                def pair(t, i, ahead=True):
                    if ahead:
                        for j in range(2):
                            low(j, t * 4 + (base - C_MIX + 2 * i + j + 3))
                    dve.wait_ge(S["chunk_used"], t * 4 + (base + 2 * i + 2))
                    x2 = xT[:, bass.ds(t * 4 + 2 * i, 2), :]
                    dve.tensor_tensor(x2, x2, PM[:, 2 * i:2 * i + 2, 0:TOK], ALU.add).then_inc(S["res_add"], 1)

                with dve.Fori(0, 3 if last else 4) as t:
                    for i in range(2):
                        pair(t, i)
                if last:
                    pair(3, 0)
                    pair(3, 1, False)

            dve.wait_ge(S["x_back"], 16)
            residual(C_WO)
            dve.wait_ge(S["res_add"], 8)
            normalise(1)
            for f in range(DFF // D):
                base = C_MLP + 32 * f
                with dve.Fori(0, 4) as t:
                    step.enter(t, 2)
                    for i in range(2):
                        for j in range(2):
                            low(j, t * 4 + (base - C_MIX + 2 * i + j + 3))
                        dve.wait_ge(S["yh_ready"], t * 2 + (8 * (f + 1) + i + 1))
                        step(dve.tensor_tensor(tr[:, i], tr[:, i], tr[:, i], ALU.mult))
                        yh, yl = (g[:, bass.ds(t * 4 + 2 * i, 2), :] for g in (YH, YL))
                        dve.tensor_tensor(yl, tr[:, i], yh, ALU.subtract).then_inc(S["yl_ready"], 1)
                    step.leave(4)
                dve.wait_ge(S["res_add"], 8 * (f + 1))
                residual(base + 16, f == DFF // D - 1)
            dve.wait_ge(S["res_add"], 40)
            normalise(2)
            for n in range(0, 12, 2):
                rows = P if n < 8 else NS
                dst = ynat[:, n // 4, 512 * (n % 4):512 * (n % 4) + 512] if n < 8 else ysam[:, 512 * (n % 4):512 * (n % 4) + 512]
                dve.wait_ge(S["y_turned"], n + 1)
                dve.tensor_copy(dst, bank(n % 4, rows=rows)).then_inc(S["y_copied"], 1)

        @block.gpsimd
        def _(pool):
            pool.wait_ge(S["prow_ready"], 1)
            for b in range(DB):
                pool.indirect_dma_start(out=rawk[b].rearrange("p a b -> p (a b)"), out_offset=None, in_=I["cache_kidx"],
                                        in_offset=bass.IndirectOffsetOnAxis(ap=prow[:, b:b + 1], axis=0)).then_inc(pages_in[b], 16)
            done = [0]

            def lows(n):
                for u in range(done[0], n):
                    pool.wait_ge(S["vh_ready"], u + 1)
                    r = raw[u // 2 % 4][:, 2 * (u % 2):2 * (u % 2) + 2, :]
                    pool.tensor_tensor(VL[:, u % 4], r, VH[:, u % 4], ALU.subtract).then_inc(S["vl_ready"], 1)
                done[0] = max(n, done[0])

            lows(UNIT * 16 + 4)
            pool.wait_ge(S["nat_done"], 14)
            pool.memset(up[:, :, 0:2], 0.0).then_inc(S["pads_zero"], 1)
            lows(UNIT * 20 + 4)
            pool.wait_ge(S["spread_read"], 1)
            pool.wait_ge(S["nat_copied"], 21)
            pool.wait_ge(S["kv_out"], 32)

            for n in range(2 * UNITS):
                src, u = ("cache_k", n) if n < UNITS else ("cache_v", n - UNITS)
                if 4 <= n < UNITS + 4:
                    pool.wait_ge(S["unit_read"], n - 3)
                elif n >= UNITS + 4:
                    pool.wait_ge(S["unit_summed"], u - 2)
                pool.indirect_dma_start(out=kv[:, n % 4, :], out_offset=None, in_=I[src],
                                        in_offset=bass.IndirectOffsetOnAxis(ap=offs[:, u:u + 1], axis=0)).then_inc(ks[n % 4], 16)
                if n < UNITS:
                    lows(UNIT * 20 + n + 1)
                elif n == UNITS + 3:
                    lows(UNIT * 36 + 4)


def constants():
    import numpy as np
    f = np.float32
    p, n32 = np.arange(P), np.arange(NS)
    c = {}
    c["ident"] = np.eye(P)
    rs = np.zeros((P, 4, P))
    for s in range(4):
        rs[:NS, s] = (p[None, :] == 4 * n32[:, None] + s)
    c["rs"] = rs.reshape(P, -1)
    c["rall"] = rs.sum(1)
    rnew = np.zeros((P, P))
    rnew[:NS] = (n32[:, None] // 4 == p[None, :] // 16) & (n32[:, None] % 4 == p[None, :] % 4)
    c["rnew"] = rnew
    c["s32"] = (p[:, None] // 4 == n32[None, :])
    c["b4"] = (p[:, None] // 4 == p[None, :] // 4)
    ok = np.zeros((P, 4))
    ok[:NS] = np.arange(4)[None, :] <= (n32 % 4)[:, None]
    c["ok4"] = ok
    c["iota"] = np.broadcast_to(np.arange(NPG), (P, NPG))
    c["tpos"] = (PAST + (p // 4) % 4)[:, None]
    c["nd"] = (np.maximum((p // 4) % 4 - p % 4, 0)[:, None] == np.arange(DT)[None, :])
    far = np.maximum(SEQ - 1 - np.arange(TW), 0)
    lo = np.array(BUCKET_LO)
    bucket = (far[None, :] >= lo[:, None]).sum(0) - 1
    oh = np.zeros((P, TW))
    oh[:NB] = bucket[None, :] == np.arange(NB)[:, None]
    c["onehot"] = oh
    am = np.zeros((P, DB, 2, IH, DT))
    for e in range(2):
        for b in range(DB):
            for t in range(DT):
                am[NS * e + DT * b + t, b, e, :, t] = 1
    c["amask"] = am.reshape(P, -1)
    pg = np.zeros((P, P))
    pg[:NPG] = np.arange(NPG)[:, None] == p[None, :] // 8
    c["pgsel"] = pg
    c["r8"] = (p % 8)[:, None]
    k = np.arange(SEQ)
    c["causal"] = np.concatenate([p[:, None] >= p[None, :], P + p[:, None] >= k[None, :]], 1)
    pack = lambda lay: np.ascontiguousarray(np.concatenate([np.asarray(c[n], f) for n, _ in lay], 1))
    return pack(CONST_P), pack(CONST_E)


_SHAPES = {"x_prompt": (SEQ, D), "x_sample": (NS, D), "cache_k": (POOL * PS, AW), "cache_v": (POOL * PS, AW),
           "cache_kidx": (POOL * 8, PS // 8 * ID), "state_conv": (DB * 2, CW), "page_table": (DB, NPG), "rel_bias": (NB, H),
           "norm_mix_g": (1, D), "w_kiwi": (P, KT * (2 * ID + IH)), "w_in": (4 * len(SEGS) + 16, P, KT * CN), "conv_w": (3, CW),
           "w_pa": (8, P, CT * CN), "w_pb": (8, P, CT * CN), "w_o": (8, P, KT * CN),
           "norm_mlp_g": (1, D), "w_mlp_in": (32, P, KT * CN), "w_mlp_out": (32, P, KT * CN), "norm_final_g": (1, D)}
_OUTS = [("y_prompt", (SEQ, D), (1, SEQ, D)), ("y_sample", (NS, D), (DB, DT, D)),
         ("k_prompt", (SEQ, AW), (1, 1, SEQ, H, HD)), ("v_prompt", (SEQ, AW), (1, 1, SEQ, H, HD)),
         ("kidx_prompt", (SEQ, ID), (1, 1, SEQ, ID)), ("conv_prompt", (2, CW), (1, 1, 2, CW)),
         ("k_sample", (NS, AW), (1, DB, DT, H, HD)), ("v_sample", (NS, AW), (1, DB, DT, H, HD)),
         ("kidx_sample", (NS, ID), (1, DB, DT, ID)), ("conv_sample", (DB * 2, CW), (1, DB, 2, CW))]


def in_tiles(w):
    rows, cols = w.shape
    kt = min(rows // P, KT)
    t = w.reshape(rows // (kt * P), kt, P, cols // CN, CN).transpose(0, 3, 2, 1, 4)
    return t.reshape(-1, P, kt * CN)


def kernel(**inputs):
    import numpy as np
    import concourse.bacc as bacc
    from concourse.bass_utils import run_bass_kernel_spmd as run

    nc = bacc.Bacc("TRN2", target_bir_lowering=False, num_devices=1)
    arrays, I = {}, {}
    w_in = inputs["w_in"][0]
    inputs = dict(inputs)
    kiwi = np.concatenate([w_in[:, KI0:KI0 + ID], w_in[:, KI0:KI0 + ID + IH]], 1)
    inputs["w_kiwi"] = kiwi.reshape(KT, P, -1).transpose(1, 0, 2)
    inputs["w_in"] = in_tiles(np.concatenate([w_in[:, c:c + 4 * CN] for c in SEGS] + [w_in[:, GA0:]], 1))
    for name in ("w_pa", "w_pb", "w_o", "w_mlp_in", "w_mlp_out"):
        inputs[name] = in_tiles(inputs[name][0])
    for name, shape in _SHAPES.items():
        arrays[name] = np.ascontiguousarray(inputs[name]).reshape(shape)
    arrays["const_p"], arrays["const_e"] = constants()
    for name, a in arrays.items():
        I[name] = nc.dram_tensor(name, a.shape, mybir.dt.from_np(a.dtype), kind="ExternalInput").ap()
    O = {name: nc.dram_tensor("out_" + name, shape, F32, kind="ExternalOutput").ap() for name, shape, _ in _OUTS}
    build(nc, I, O)
    r = run(nc, [arrays], core_ids=[0])
    return tuple(r.results[0]["out_" + name].reshape(shape) for name, _, shape in _OUTS)
```
